# Optimizing a Trainium2 kernel written in Bass

```python
import math
import jax, jax.numpy as jnp
from jax import lax
import numpy as np

D_MODEL = 1024
BATCH = 1
SEQ = 512
DEPTH = 1

HEAD_DIM = 64
N_ATTN_HEADS = 8
ATTN_WIDTH = N_ATTN_HEADS * HEAD_DIM
N_RWKV_HEADS = 8
RWKV_WIDTH = N_RWKV_HEADS * HEAD_DIM
MIX_WIDTH = ATTN_WIDTH + RWKV_WIDTH
RWKV_DECAY_LORA = 32
RWKV_AAA_LORA = 32
RWKV_GATE_LORA = 96
RWKV_SHIFT_WIDTH = 3 * RWKV_WIDTH + RWKV_DECAY_LORA + RWKV_AAA_LORA + RWKV_GATE_LORA
IN_PROJ_WIDTH = 3 * ATTN_WIDTH + RWKV_SHIFT_WIDTH
RWKV_DECAY_SCALE = math.exp(-0.5)
RWKV_GN_EPS = HEAD_DIM * 1e-5
MOBA_BLOCK = 256
MOBA_TOPK = 3
MOBA_QCHUNK = 32
N_EXPERTS = 32
TOP_K = 4
D_EXPERT = D_MODEL
SWIGLU_LIMIT = 7.0
SWIGLU_ALPHA = 1.702
MOE_BLOCK = 256
NORM_EPS = 1e-6
NEG_INF = -1e30

kernel_name = "hymba_moba_rwkv7_gptoss_moe_block"

def rms_norm(x, g):
    xf = x.astype(jnp.float32)
    return xf * lax.rsqrt(jnp.mean(xf * xf, axis=-1, keepdims=True) + NORM_EPS) * g.astype(jnp.float32)

def alibi_slopes(n_heads):
    return 2.0 ** (-8.0 * jnp.arange(1, n_heads + 1, dtype=jnp.float32) / n_heads)

def moba_attention(q, k, v, slopes):
    B, S, H, Dh = q.shape
    Sp = -(-S // MOBA_BLOCK) * MOBA_BLOCK
    pad = ((0, 0), (0, Sp - S), (0, 0), (0, 0))
    q, k, v = [jnp.pad(t, pad).transpose(0, 2, 1, 3) for t in (q, k, v)]
    nb = Sp // MOBA_BLOCK
    n_sel = min(MOBA_TOPK, nb)
    n_chunks = Sp // MOBA_QCHUNK
    kb = k.reshape(B, H, nb, MOBA_BLOCK, Dh)
    vb = v.reshape(B, H, nb, MOBA_BLOCK, Dh)
    k_mean = kb.mean(axis=3)
    q_chunks = q.reshape(B, H, n_chunks, MOBA_QCHUNK, Dh).transpose(2, 0, 1, 3, 4)
    scale = Dh ** -0.5
    b_idx = jnp.arange(B)[:, None, None, None]
    h_idx = jnp.arange(H)[None, :, None, None]
    key_off = jnp.arange(MOBA_BLOCK)

    def attend_chunk(args):
        qq, ci = args
        t = ci * MOBA_QCHUNK + jnp.arange(MOBA_QCHUNK)
        own = (ci * MOBA_QCHUNK) // MOBA_BLOCK
        gate = jnp.einsum('bhqd,bhnd->bhqn', qq, k_mean)
        gate = jnp.where(jnp.arange(nb) < own, gate, NEG_INF)
        _, sel = lax.top_k(gate, n_sel)
        sel_valid = jnp.arange(n_sel) < own
        k_sel = kb[b_idx, h_idx, sel]
        v_sel = vb[b_idx, h_idx, sel]
        pos_sel = sel[..., None] * MOBA_BLOCK + key_off
        dist_sel = (t[None, None, :, None, None] - pos_sel).astype(jnp.float32)
        s_sel = (jnp.einsum('bhqd,bhqnkd->bhqnk', qq, k_sel) * scale
                 - slopes[None, :, None, None, None] * dist_sel)
        s_sel = jnp.where(sel_valid[:, None], s_sel, NEG_INF)
        k_own = lax.dynamic_index_in_dim(kb, own, axis=2, keepdims=False)
        v_own = lax.dynamic_index_in_dim(vb, own, axis=2, keepdims=False)
        pos_own = own * MOBA_BLOCK + key_off
        dist_own = (t[:, None] - pos_own[None, :]).astype(jnp.float32)
        s_own = (jnp.einsum('bhqd,bhkd->bhqk', qq, k_own) * scale
                 - slopes[None, :, None, None] * dist_own[None, None])
        s_own = jnp.where(dist_own >= 0, s_own, NEG_INF)
        scores = jnp.concatenate([s_sel.reshape(B, H, MOBA_QCHUNK, n_sel * MOBA_BLOCK), s_own], axis=-1)
        p = jax.nn.softmax(scores.astype(jnp.float32), axis=-1)
        p_sel = p[..., :n_sel * MOBA_BLOCK].reshape(B, H, MOBA_QCHUNK, n_sel, MOBA_BLOCK)
        p_own = p[..., n_sel * MOBA_BLOCK:]
        return (jnp.einsum('bhqnk,bhqnkd->bhqd', p_sel, v_sel)
                + jnp.einsum('bhqk,bhkd->bhqd', p_own, v_own))

    out = lax.map(attend_chunk, (q_chunks, jnp.arange(n_chunks)))
    out = out.transpose(1, 0, 3, 2, 4).reshape(B, Sp, H, Dh)
    return out[:, :S]

def rwkv7_time_mix(xr, mu, w0, w2, a0, a2, g2, k_k, k_a, r_k, ln_g, ln_b):
    B, S, _ = xr.shape
    H, N = N_RWKV_HEADS, HEAD_DIM
    x_prev = jnp.pad(xr, ((0, 0), (1, 0), (0, 0)))[:, :S]
    xs = xr + (x_prev - xr) * mu
    o1 = RWKV_WIDTH
    o2 = 2 * RWKV_WIDTH
    o3 = 3 * RWKV_WIDTH
    o4 = o3 + RWKV_DECAY_LORA
    o5 = o4 + RWKV_AAA_LORA
    r, k, v, dw, da, dg = jnp.split(xs, [o1, o2, o3, o4, o5], axis=-1)
    w = jnp.exp(-RWKV_DECAY_SCALE * jax.nn.sigmoid(w0 + jnp.tanh(dw) @ w2))
    a = jax.nn.sigmoid(a0 + da @ a2)
    g = jax.nn.sigmoid(dg) @ g2
    heads = lambda t: t.reshape(B, S, H, N)
    kk = heads(k * k_k)
    kk = kk * lax.rsqrt(jnp.maximum(jnp.sum(kk * kk, axis=-1, keepdims=True), 1e-24))
    k = k * (1.0 + (a - 1.0) * k_a)
    r, w, k, v, a = [heads(t) for t in (r, w, k, v, a)]
    b_vec = kk * a
    seq_first = lambda t: t.transpose(1, 0, 2, 3)

    def step(state, inp):
        r_t, w_t, k_t, v_t, kk_t, b_t = inp
        sa = jnp.einsum('bhvk,bhk->bhv', state, -kk_t)
        state = (state * w_t[:, :, None, :] + sa[..., None] * b_t[:, :, None, :]
                 + v_t[..., None] * k_t[:, :, None, :])
        return state, jnp.einsum('bhvk,bhk->bhv', state, r_t)

    state0 = jnp.zeros((B, H, N, N), jnp.float32)
    xs_scan = tuple(seq_first(t.astype(jnp.float32)) for t in (r, w, k, v, kk, b_vec))
    _, o = lax.scan(step, state0, xs_scan)
    o = seq_first(o)
    mean = jnp.mean(o, axis=-1, keepdims=True)
    var = jnp.mean(jnp.square(o - mean), axis=-1, keepdims=True)
    o = ((o - mean) * lax.rsqrt(var + RWKV_GN_EPS)).reshape(B, S, RWKV_WIDTH) * ln_g + ln_b
    bonus = jnp.sum(r * k * r_k, axis=-1, keepdims=True) * v
    return (o + bonus.reshape(B, S, RWKV_WIDTH)) * g

def moe_ffn(xn, w_router, b_router, w_gate, b_gate, w_up, b_up, w_down, b_down):
    T, D = xn.shape
    logits = (xn @ w_router + b_router).astype(jnp.float32)
    top_val, top_idx = lax.top_k(logits, TOP_K)
    gates = jax.nn.softmax(top_val, axis=-1)
    A = T * TOP_K
    e_flat = top_idx.reshape(A)
    tok_flat = jnp.arange(A) // TOP_K
    g_flat = gates.reshape(A)
    order = jnp.argsort(e_flat)
    e_sorted = e_flat[order]
    tok_sorted = tok_flat[order]
    g_sorted = g_flat[order]
    counts = jnp.bincount(e_flat, length=N_EXPERTS)
    padded = ((counts + MOE_BLOCK - 1) // MOE_BLOCK) * MOE_BLOCK
    pad_end = jnp.cumsum(padded)
    pad_start = pad_end - padded
    grp_start = jnp.cumsum(counts) - counts
    dest = pad_start[e_sorted] + (jnp.arange(A) - grp_start[e_sorted])
    n_blocks = -(-A // MOE_BLOCK) + N_EXPERTS
    P = n_blocks * MOE_BLOCK
    slot_tok = jnp.full((P,), T, dtype=jnp.int32).at[dest].set(tok_sorted.astype(jnp.int32))
    block_expert = jnp.minimum(
        jnp.searchsorted(pad_end, jnp.arange(n_blocks) * MOE_BLOCK, side='right'), N_EXPERTS - 1)
    x_pad = jnp.concatenate([xn, jnp.zeros((1, D), xn.dtype)], axis=0)

    def expert_block(args):
        toks, e = args
        h = x_pad[toks]
        gate = jnp.minimum(h @ w_gate[e] + b_gate[e], SWIGLU_LIMIT)
        up = jnp.clip(h @ w_up[e] + b_up[e], -SWIGLU_LIMIT, SWIGLU_LIMIT)
        glu = gate * jax.nn.sigmoid(SWIGLU_ALPHA * gate)
        return ((up + 1.0) * glu) @ w_down[e] + b_down[e]

    y_slots = lax.map(expert_block, (slot_tok.reshape(n_blocks, MOE_BLOCK), block_expert)).reshape(P, D)
    return jax.ops.segment_sum(y_slots[dest] * g_sorted[:, None], tok_sorted, num_segments=T)

def setup_inputs(seed: int = 0) -> dict:
    key = jax.random.key(seed)
    ks = jax.random.split(key, 32)
    L, D, E, F = DEPTH, D_MODEL, N_EXPERTS, D_EXPERT
    nrm = lambda k, shape, s: jax.random.normal(k, shape, jnp.float32) * s
    return {
        "x": nrm(ks[0], (BATCH, SEQ, D), 1.0),
        "norm_mix_g": 1.0 + nrm(ks[1], (L, D), 0.05),
        "w_in": nrm(ks[2], (L, D, IN_PROJ_WIDTH), D ** -0.5),
        "attn_norm_g": 1.0 + nrm(ks[3], (L, ATTN_WIDTH), 0.05),
        "rwkv_mu": jax.random.uniform(ks[4], (L, RWKV_SHIFT_WIDTH), jnp.float32),
        "rwkv_w0": nrm(ks[5], (L, RWKV_WIDTH), 0.5),
        "rwkv_w2": nrm(ks[6], (L, RWKV_DECAY_LORA, RWKV_WIDTH), 0.1),
        "rwkv_a0": nrm(ks[7], (L, RWKV_WIDTH), 0.1),
        "rwkv_a2": nrm(ks[8], (L, RWKV_AAA_LORA, RWKV_WIDTH), 0.1),
        "rwkv_g2": nrm(ks[9], (L, RWKV_GATE_LORA, RWKV_WIDTH), RWKV_GATE_LORA ** -0.5),
        "rwkv_k_k": 0.85 + nrm(ks[10], (L, RWKV_WIDTH), 0.05),
        "rwkv_k_a": 1.0 + nrm(ks[11], (L, RWKV_WIDTH), 0.05),
        "rwkv_r_k": nrm(ks[12], (L, N_RWKV_HEADS, HEAD_DIM), 0.1),
        "rwkv_ln_g": 1.0 + nrm(ks[13], (L, RWKV_WIDTH), 0.05),
        "rwkv_ln_b": nrm(ks[14], (L, RWKV_WIDTH), 0.01),
        "w_out": nrm(ks[15], (L, MIX_WIDTH, D), MIX_WIDTH ** -0.5),
        "norm_ffn_g": 1.0 + nrm(ks[16], (L, D), 0.05),
        "w_router": nrm(ks[17], (L, D, E), D ** -0.5),
        "b_router": nrm(ks[18], (L, E), 0.01),
        "moe_w_gate": nrm(ks[19], (L, E, D, F), D ** -0.5),
        "moe_b_gate": nrm(ks[20], (L, E, F), 0.01),
        "moe_w_up": nrm(ks[21], (L, E, D, F), D ** -0.5),
        "moe_b_up": nrm(ks[22], (L, E, F), 0.01),
        "moe_w_down": nrm(ks[23], (L, E, F, D), F ** -0.5),
        "moe_b_down": nrm(ks[24], (L, E, D), 0.01),
        "norm_final_g": 1.0 + nrm(ks[25], (D,), 0.05),
    }

def reference(x, norm_mix_g, w_in, attn_norm_g, rwkv_mu, rwkv_w0, rwkv_w2, rwkv_a0, rwkv_a2,
              rwkv_g2, rwkv_k_k, rwkv_k_a, rwkv_r_k, rwkv_ln_g, rwkv_ln_b, w_out, norm_ffn_g,
              w_router, b_router, moe_w_gate, moe_b_gate, moe_w_up, moe_b_up, moe_w_down,
              moe_b_down, norm_final_g):
    B, S, D = x.shape
    slopes = alibi_slopes(N_ATTN_HEADS)
    h = x.astype(jnp.float32)
    for l in range(DEPTH):
        xn = rms_norm(h, norm_mix_g[l])
        proj = xn @ w_in[l]
        q = proj[..., :ATTN_WIDTH].reshape(B, S, N_ATTN_HEADS, HEAD_DIM)
        k = proj[..., ATTN_WIDTH:2 * ATTN_WIDTH].reshape(B, S, N_ATTN_HEADS, HEAD_DIM)
        v = proj[..., 2 * ATTN_WIDTH:3 * ATTN_WIDTH].reshape(B, S, N_ATTN_HEADS, HEAD_DIM)
        o_att = moba_attention(q, k, v, slopes)
        o_att = o_att * lax.rsqrt(jnp.mean(o_att * o_att, axis=-1, keepdims=True) + NORM_EPS)
        o_att = o_att.reshape(B, S, ATTN_WIDTH) * attn_norm_g[l]
        o_rwkv = rwkv7_time_mix(proj[..., 3 * ATTN_WIDTH:], rwkv_mu[l], rwkv_w0[l], rwkv_w2[l],
                                rwkv_a0[l], rwkv_a2[l], rwkv_g2[l], rwkv_k_k[l], rwkv_k_a[l],
                                rwkv_r_k[l], rwkv_ln_g[l], rwkv_ln_b[l])
        h = h + jnp.concatenate([o_att, o_rwkv], axis=-1) @ w_out[l]
        xn2 = rms_norm(h, norm_ffn_g[l]).reshape(B * S, D)
        y = moe_ffn(xn2, w_router[l], b_router[l], moe_w_gate[l], moe_b_gate[l],
                    moe_w_up[l], moe_b_up[l], moe_w_down[l], moe_b_down[l])
        h = h + y.reshape(B, S, D)
    return rms_norm(h, norm_final_g).astype(x.dtype)


_drawn_inputs = setup_inputs


def setup_inputs(seed=0):
    import zlib

    import numpy as np

    out = dict(_drawn_inputs(seed))
    spreads = {}
    factors = {'rwkv_k_k': 15.085,
     'rwkv_ln_b': 5.495,
     'b_router': 2.725,
     'moe_b_gate': 8.0,
     'moe_b_up': 22.06,
     'moe_b_down': 8.0}
    for name, (base, spread) in spreads.items():
        noise = np.random.default_rng([zlib.crc32(name.encode()), seed]).standard_normal(out[name].shape)
        drawn = base * np.exp(spread * noise) if base else spread * noise
        out[name] = __import__('jax').numpy.asarray(drawn.astype(out[name].dtype))
    for name, factor in factors.items():
        out[name] = (out[name] * factor).astype(out[name].dtype)
    return out
```

```python
import math
from contextlib import ExitStack

import concourse.bass as bass
from concourse import mybir


def hymba_block(nc, t_in, out):
    F32, F32R, BF16 = mybir.dt.float32, mybir.dt.float32r, mybir.dt.bfloat16
    I32, U32 = mybir.dt.int32, mybir.dt.uint32
    ALU = mybir.AluOpType
    ACT = mybir.ActivationFunctionType
    AXX = mybir.AxisListType.X
    ds = bass.ds

    P = 128
    D, SEQ, HD = 1024, 512, 64
    TT = SEQ // P
    KT = D // P
    HP = 4
    CH = 64
    NE, TOPK = 32, 4
    NB = SEQ * TOPK // P + NE
    C = 1024
    NRAW, NHL = 6, 4
    NRAW2, NHL2 = 12, 8
    IN_CH, OUT_CH = 26, 8
    MOE0 = IN_CH + OUT_CH
    PER = 24
    DECAY = math.exp(-0.5)
    EPS, GN_EPS = 1e-6, HD * 1e-5
    LIMIT, ALPHA = 7.0, 1.702
    SKIP = 1.0e6
    NBT = NB + 2

    MU, W0, A0, KK_, KA_, RK_, LNG, LNB, ATG = 0, 14, 18, 22, 26, 30, 34, 38, 42
    NPAR = 17

    x_d = t_in["x"][0]
    w_in_v = t_in["w_in"][0].rearrange("(p k) n -> p k n", k=KT)
    w_out_v = t_in["w_out"][0].rearrange("(c p) n -> p c n", p=P)
    wg_v = t_in["moe_w_gate"].rearrange("l e (p k) f -> (l e) p (k f)", k=KT)
    wu_v = t_in["moe_w_up"].rearrange("l e (p k) f -> (l e) p (k f)", k=KT)
    wd_v = t_in["moe_w_down"].rearrange("l e (p k) f -> (l e) p (k f)", k=KT)

    ctx = ExitStack()

    def sb(name, shape, dt=F32, scope=None):
        return (scope or ctx).enter_context(nc.sbuf_tensor(name, shape, dt))

    def sem(name):
        return ctx.enter_context(nc.semaphore(name))

    with ctx:
        pair = [ctx.enter_context(nc.psum_tensor(f"banks{2 * i}_{2 * i + 1}", [P, 1024], F32)) for i in range(4)]
        bank = [pair[i // 2][:, (i % 2) * 512:(i % 2) * 512 + 512] for i in range(8)]

        H = sb("residual", [P, TT, D])
        biasb = sb("expert_bias_parts", [96, 3, D], BF16)
        ident = sb("ident", [P, P])
        ss = sb("sum_squares", [P, 3 * TT])
        rms = sb("rms_scale", [P, 3 * TT])
        neghalf = sb("neg_half", [P, 1])
        iota32 = sb("iota_experts", [P, NE])
        onesf = sb("ones_experts", [P, NE])
        b_rout = sb("b_router_rows", [P, NE])
        w_rout = sb("w_router", [P, KT, NE])
        triu = sb("tri_strict", [P, P], BF16)
        ones_b = sb("ones_b", [P, P], BF16)
        iotaB = sb("iota_blocks", [P, NBT])
        iotaR = sb("iota_rows", [P, P])
        pair_ids = sb("pair_ids", [P, 3, TT * TOPK])
        lane32 = sb("lane_mod_32", [P, 1])
        blk_exp = sb("block_expert", [P, NBT], I32)
        n_blk = sb("n_blocks", [P, 2], I32)
        expsel = sb("expert_selector", [96, NBT], BF16)
        idx_x = sb("slot_token", [P, NBT], I32)
        idx_y = sb("slot_pair", [P, NBT], I32)
        gates = sb("gates", [P, TT, TOPK])

        pre = ExitStack()
        raw = sb("w_raw", [P, NRAW, C], scope=pre)
        whi = sb("w_hi", [P, NHL, C], F32R, scope=pre)
        wlo = sb("w_lo", [P, NHL, C], F32R, scope=pre)
        par_rows = sb("param_rows", [48, P], scope=pre)
        par = sb("params", [P, 48], scope=pre)
        one_m_ka = sb("one_minus_k_a", [P, HP], scope=pre)
        g_mix = sb("norm_mix_g", [P, KT], scope=pre)
        w2a2 = sb("w2_a2", [64, 512], scope=pre)
        g2 = sb("g2", [96, 512], scope=pre)
        head_ones = sb("head_ones", [P, P], scope=pre)
        mask_su = sb("mask_s_lt_t", [P, P], scope=pre)
        mask_iu = sb("mask_s_le_t", [P, P], scope=pre)
        lvl = sb("level_masks", [P, 6, P], scope=pre)
        lvl0T = sb("level0_mask_T", [P, P], scope=pre)
        dist = sb("minus_distance", [P, 512], scope=pre)
        SCM = sb("scan_mult", [P, 8 * 65], scope=pre)
        RX = sb("r_shifted", [P, HP, 512], scope=pre)
        KX = sb("k_shifted", [P, HP, 512], scope=pre)
        VX = sb("v_shifted", [P, HP, 512], scope=pre)
        XL = sb("lora_shifted", [P, 2, 512], scope=pre)
        xs = sb("x_scaled", [P, 2, D], scope=pre)
        MA = xs[:, :, :].rearrange("p a (b t) -> p (a b) t", b=2)

        q_scope = ExitStack()
        QT = sb("qT", [P, HP, 512], scope=q_scope)
        KTT = sb("kT", [P, HP, 512], scope=q_scope)
        VA = sb("v_att", [P, TT, 512], scope=q_scope)
        a_scope = ExitStack()
        xnh = sb("xn_hi", [P, KT, 512], F32R, scope=a_scope)
        xnl = sb("xn_lo", [P, KT, 512], F32R, scope=a_scope)
        XR = sb("x_unshifted", [P, 2, 513], scope=a_scope)
        DF = sb("x_shift_diff", [P, 2, 512], scope=a_scope)
        bias_raw = sb("expert_bias_words", [96, D], scope=a_scope)
        a_scope.close()
        SC = sb("scores", [P, 2, 2, 512], scope=q_scope)
        PR = sb("probs", [P, 2, 2, 512], scope=q_scope)
        PRT = sb("probs_T", [P, 2, 2, 512], scope=q_scope)
        nmax = sb("neg_row_max", [P, 32], scope=q_scope)
        rsum = sb("row_sum", [P, 32], scope=q_scope)
        rinv = sb("row_rinv", [P, 32], scope=q_scope)
        ON = sb("att_norm", [P, 8, HD], scope=q_scope)
        OSQ = sb("att_sq", [P, 8, HD], scope=q_scope)
        hss = sb("att_head_ss", [P, TT, 8], scope=q_scope)
        hrs = sb("att_head_rms", [P, TT, 8], scope=q_scope)
        q_scope.close()

        r_scope = ExitStack()
        KKN = sb("minus_kk", [P, HP, 512], scope=r_scope)
        BV = sb("b_vec", [P, HP, 512], scope=r_scope)
        CS = sb("decay_cumsum", [P, HP, 8, CH + 1], scope=r_scope)
        p_scope = ExitStack()
        SIG = sb("decay_sigmoid", [P, HP, 8, CH + 1], scope=p_scope)
        TL = sb("tanh_lora", [32, 512], scope=p_scope)
        AV = sb("a_vec", [P, HP, 512], scope=p_scope)
        T1 = sb("k_factor", [P, 2, 512], scope=p_scope)
        T2 = sb("kk_ss", [P, 2, 512], scope=p_scope)
        T3 = sb("kk_scale", [P, 2, 512], scope=p_scope)
        T4 = sb("kk_sq", [P, 2, 512], scope=p_scope)
        T5 = sb("kk_newton", [P, 512], scope=p_scope)
        p_scope.close()
        l_scope = ExitStack()
        E01 = sb("exp_cs", [P, HP, 2, CH + 1], scope=l_scope)
        EI = sb("exp_neg_cs", [P, HP, 2, CH], scope=l_scope)
        ASt = sb("a_tile", [P, HP, P], scope=l_scope)
        BSt = sb("b_tile", [P, HP, P], scope=l_scope)
        KSt = sb("k_tile", [P, HP, P], scope=l_scope)
        RSt = sb("r_tile", [P, HP, P], scope=l_scope)
        VSt = sb("v_tile", [P, HP, P], scope=l_scope)
        BP = sb("bonus_product", [P, HP, P], scope=l_scope)
        Bt = sb("b_rows", [P, 512], scope=l_scope)
        Kt = sb("k_rows", [P, 512], scope=l_scope)
        Vt = sb("v_rows", [P, 512], scope=l_scope)
        AZ = sb("a_z0_rows", [P, 8, 2, CH], scope=l_scope)
        TKm = sb("TK_T", [P, 2, HP, P], scope=l_scope)
        RBm = sb("RB_T", [P, 2, HP, P], scope=l_scope)
        RKm = sb("RK_T", [P, 2, HP, P], scope=l_scope)
        UZ = sb("u_z_rows", [P, 2, 8, CH], scope=l_scope)
        R2 = sb("r2_T", [P, HP, P], scope=l_scope)
        SN = sb("state_sum", [P, HP, P], scope=l_scope)
        ST = sb("state_T", [P, HP, P], scope=l_scope)
        l_scope.close()
        AsT, Xi, XiT, Pm = (H[:, k, :].rearrange("p (j h t) -> p j h t", j=2, h=HP) for k in range(4))
        MTm, NN = Pm, AsT
        r_scope.close()
        o_scope = ExitStack()
        G = sb("gate_T", [P, HP, 512], scope=o_scope)
        U1 = sb("gn_centered", [P, 2, 512], scope=o_scope)
        U2 = sb("gn_sq", [P, 2, 512], scope=o_scope)
        U3 = sb("gn_scale", [P, 2, 512], scope=o_scope)
        U4 = sb("gn_newton", [P, 512], scope=o_scope)
        mxh = sb("mix_hi", [P, 8, 512], F32R, scope=o_scope)
        mxl = sb("mix_lo", [P, 8, 512], F32R, scope=o_scope)
        o_scope.close()
        pre.close()

        g_ffn = sb("norm_ffn_g", [P, D])
        rt = ExitStack()
        XN2 = sb("xn2", [P, TT, D], scope=rt)
        X2T = sb("xn2_T", [P, KT, 512], scope=rt)
        LG = sb("logits", [P, TT, NE], scope=rt)
        top8 = sb("top8", [P, TT, 8], scope=rt)
        idx8 = sb("idx8", [P, TT, 8], U32, scope=rt)
        idx8f = sb("idx8f", [P, TT, 8], scope=rt)
        OH = sb("onehot", [P, TT, TOPK, NE], scope=rt)
        MB = sb("member", [P, TT, NE], BF16, scope=rt)
        gsum = sb("gate_sum", [P, TT], scope=rt)
        ntop = sb("neg_top", [P, TT], scope=rt)
        rgs = sb("gate_rsum", [P, TT], scope=rt)
        nbv = sb("blocks_parts", [P, 4, NE], scope=rt)
        nbl = sb("blocks_of_expert", [P, NE], scope=rt)
        bend = sb("block_end", [P, NE], scope=rt)
        bst = sb("slot_start", [P, NE], scope=rt)
        rank = sb("slot_of_expert", [P, TT, NE], scope=rt)
        dtmp = sb("dest_parts", [P, TT, TOPK, NE], scope=rt)
        dest = sb("dest", [P, TT * TOPK], scope=rt)
        destb = sb("dest_block", [P, TT * TOPK], scope=rt)
        destr = sb("dest_row", [P, TT * TOPK], scope=rt)
        dcmp = sb("dest_cmp", [P, TT * TOPK, NBT], scope=rt)
        iotaBx = sb("iota_128_blocks", [P, NBT], scope=rt)
        ohR = sb("onehot_row", [P, TT * TOPK, P], BF16, scope=rt)
        rhsv = sb("pair_value", [P, 3, TT * TOPK, NBT], BF16, scope=rt)
        ecmp = sb("expert_cmp", [P, NBT, NE], scope=rt)
        bef = sb("block_expert_f", [P, NBT], scope=rt)
        slotv = sb("slot_value", [P, 2, NBT], scope=rt)
        skipv = sb("slot_skip", [P, NBT], scope=rt)
        rt.close()

        mo = ctx.enter_context(ExitStack())
        raw2 = sb("expert_w_raw", [P, NRAW2, C], scope=mo)
        whi2 = sb("expert_w_hi", [P, NHL2, C], F32R, scope=mo)
        wlo2 = sb("expert_w_lo", [P, NHL2, C], F32R, scope=mo)
        XB = sb("x_block", [P, 2, D], scope=mo)
        xbh = [sb(f"x_block_T_hi{q}", [P, KT, P], F32R, scope=mo) for q in range(2)]
        xbl = [sb(f"x_block_T_lo{q}", [P, KT, P], F32R, scope=mo) for q in range(2)]
        now_x = [sb(f"gather_rows{q}", [P, 1], I32, scope=mo) for q in range(2)]
        now_y = sb("scatter_rows", [P, 1], I32, scope=mo)
        bsel = sb("bias_selector", [96, P], BF16, scope=mo)
        GT = sb("gate_act", [P, D], scope=mo)
        SG = sb("gate_sigmoid", [P, D], scope=mo)
        UP = sb("up_act", [P, D], scope=mo)
        HB = sb("h_block", [P, D], scope=mo)
        hbh = sb("h_block_T_hi", [P, KT, P], F32R, scope=mo)
        hbl = sb("h_block_T_lo", [P, KT, P], F32R, scope=mo)
        YB = sb("y_block", [P, D], scope=mo)
        YG = raw2[:, 0:2 * TOPK, :].rearrange("p (a k) d -> p a k d", a=2)
        g_fin = sb("norm_final_g", [P, D], scope=mo)
        FO = XB

        xn2_d = nc.dram_tensor("xn2_rows", (SEQ, D), F32, kind="Internal").ap()
        y_d = nc.dram_tensor("y_pair_rows", (SEQ * TOPK, D), F32, kind="Internal").ap()

        sems = {}

        def S(name):
            if name not in sems:
                sems[name] = ctx.enter_context(nc.semaphore(name))
            return sems[name]

        class Chain:

            def __init__(self, eng, name):
                self.eng, self.sem, self.base, self.n = eng, S(name), 0, 0

            def link(self, ins):
                self.n += 1
                ins.then_inc(self.sem, 1)
                self.eng.wait_ge(self.sem, self.base + self.n)

        hi_done, lo_done, w_used = S("hi_done"), S("lo_done"), S("weights_used")

        class Ring:

            def __init__(self, raw_, hi_, lo_, nraw, nhl, start, before):
                self.raw, self.hi, self.lo, self.nraw, self.nhl = raw_, hi_, lo_, nraw, nhl
                self.landed = [S(f"weights_in_{i}") for i in range(nraw)]
                self.start = start
                self.before = before

            def load(self, sp, n, k, src, view=None):
                if not isinstance(n, int) or n >= self.start + self.nraw:
                    sp.wait_ge(lo_done, n - (self.nraw - 1))
                dst = self.raw[:, k % self.nraw, :]
                sp.dma_start(dst if view is None else view(dst), src).then_inc(self.landed[k % self.nraw], 16)

            def make_hi(self, act, n, k, turn, width=C):
                act.wait_ge(self.landed[k % self.nraw], 16 * (turn + 1 + self.before[k % self.nraw]))
                if not isinstance(n, int) or n >= self.start + self.nhl:
                    act.wait_ge(w_used, n - (self.nhl - 1))
                act.activation(self.hi[:, k % self.nhl, 0:width], self.raw[:, k % self.nraw, 0:width], ACT.Copy)\
                    .then_inc(hi_done, 1)

            def make_lo(self, dve, n, k, width=C):
                dve.wait_ge(hi_done, n + 1)
                dve.tensor_tensor(self.lo[:, k % self.nhl, 0:width], self.raw[:, k % self.nraw, 0:width],
                                  self.hi[:, k % self.nhl, 0:width].bitcast(F32), ALU.subtract).then_inc(lo_done, 1)

        ring = Ring(raw, whi, wlo, NRAW, NHL, 0, [0] * NRAW)
        xring = Ring(raw2, whi2, wlo2, NRAW2, NHL2, MOE0,
                     [len(range(i, MOE0, NRAW)) if i < NRAW else 0 for i in range(NRAW2)])

        def in_width(n):
            return C if n < 24 else 4 * 160

        def hi_range(act, a, b):
            for n in range(a, b):
                ring.make_hi(act, n, n, n // NRAW, in_width(n) if n < IN_CH else C)

        def lo_range(dve, a, b):
            for n in range(a, b):
                ring.make_lo(dve, n, n, in_width(n) if n < IN_CH else C)

        def three(pe, o, wh, wl, xh, xl, start, stop, w_moving):
            for t, (w, x) in enumerate(((wh, xh), (wh, xl), (wl, xh))):
                lhs, rhs = (x, w) if w_moving else (w, x)
                last = pe.matmul(o, lhs, rhs, start=start and t == 0, stop=stop and t == 2)
            return last

        def bc(ap, shape, axis):
            return ap.unsqueeze(axis).to_broadcast(shape)

        eye4 = bc(ident[:, :], [P, HP, P], 1)

        def tiles(ap, tt):
            return ap[:, :, ds(tt * P, P)]

        def tile_chunks(ap, tt):
            return ap.rearrange("p h (c t) -> p h c t", t=CH)[:, :, ds(tt * 2, 2), :]

        block = ctx.enter_context(nc.Block())

        @block.sync
        def _(sp):
            for tt in range(TT):
                sp.dma_start(H[:, tt, :], x_d[tt * P:(tt + 1) * P, :]).then_inc(S("x_in"), 16)
            for n in range(IN_CH):
                if n < 24:
                    g, q = n // 4, n % 4
                    ring.load(sp, n, n, w_in_v[:, 2 * q:2 * q + 2, 512 * g:512 * g + 512],
                               lambda r: r.rearrange("p (k n) -> p k n", k=2))
                else:
                    q = n - 24
                    ring.load(sp, n, n, w_in_v[:, 4 * q:4 * q + 4, 3072:3232],
                               lambda r: r[:, 0:640].rearrange("p (k n) -> p k n", k=4))
            for c in range(OUT_CH):
                ring.load(sp, IN_CH + c, IN_CH + c, w_out_v[:, c, :])
            sp.wait_ge(S("state_written"), 2 * TT + 1)
            sp.wait_ge(S("rwkv_out"), TT)
            for tt in range(TT):
                sp.dma_start(H[:, tt, :], x_d[tt * P:(tt + 1) * P, :]).then_inc(S("x_in"), 16)
            sp.wait_ge(S("mix_added"), 8)
            sp.dma_start(g_ffn[:, :], t_in["norm_ffn_g"][0].partition_broadcast(P)).then_inc(S("g_ffn_in"), 16)
            for tt in range(TT):
                sp.wait_ge(S("xn2_ok"), tt + 1)
                sp.dma_start(xn2_d[tt * P:(tt + 1) * P, :], XN2[:, tt, :]).then_inc(S("xn2_stored"), 16)

            def chunk_src(w, e, c):
                return w[ds(e, 1), :, c * C:(c + 1) * C].rearrange("o p n -> (o p) n")

            sp.wait_ge(S("tables_ok"), 1)
            nb = sp.value_load(n_blk[0:1, 0:1], min_val=16, max_val=NB - 1)
            sp.wait_ge(S("xn2_stored"), 16 * TT)
            sp.dma_start(g_fin[:, :], t_in["norm_final_g"].partition_broadcast(P)).then_inc(S("g_fin_in"), 16)
            e0 = sp.value_load(blk_exp[0:1, 0:1], min_val=0, max_val=NE - 1)
            for c in range(8):
                xring.load(sp, MOE0 + c, c, chunk_src(wg_v, e0, c))

            def block_loads(i):
                e = sp.value_load(blk_exp[0:1, ds(i, 1)], min_val=0, max_val=NE - 1)
                en = sp.value_load(blk_exp[0:1, ds(i + 1, 1)], min_val=0, max_val=NE - 1)
                base = MOE0 + 8 + i * PER
                for k, (w, ex) in enumerate(((wu_v, e), (wg_v, en), (wd_v, e))):
                    for c in range(8):
                        xring.load(sp, base + (8 * k + c), 8 + 8 * k + c, chunk_src(w, ex, c))

            block_loads(0)
            block_loads(1)
            with sp.Fori(0, (NB - 2) // 2) as it:
                for q in range(2):
                    i = it * 2 + (2 + q)
                    with sp.If(i < nb):
                        block_loads(i)
            sp.wait_ge(S("y_stored"), nb * 16)
            for tt in range(TT):
                if tt >= 2:
                    sp.wait_ge(S("combined"), tt - 1)
                sp.dma_start(YG[:, tt % 2, :, :],
                             y_d[tt * P * TOPK:(tt + 1) * P * TOPK, :].rearrange("(p k) d -> p k d", k=TOPK))\
                    .then_inc(S(f"y_pairs_in{tt % 2}"), 16)
            for tt in range(TT):
                sp.wait_ge(S("final_ok"), tt + 1)
                sp.dma_start(out[0, tt * P:(tt + 1) * P, :], FO[:, tt % 2, :]).then_inc(S("out_stored"), 16)
                if tt < TT - 2:
                    sp.wait_ge(S("out_stored"), 16 * (tt + 1))
                    sp.sem_inc(S("final_free"), 1)
            sp.wait_ge(S("out_stored"), 16 * TT)
            sp.wait_ge(S("xn2_stored"), 16 * TT)

        @block.gpsimd
        def _(pool):
            ch = Chain(pool, "pool_chain")
            pool.memset(par_rows[:, :], 0.0).then_inc(S("param_rows_zero"), 1)
            pool.memset(XR[:, :, 0:1], 0.0).then_inc(S("zero_columns"), 1)

            def keep(buf, view, pattern, base, cm, op, fill=0.0):
                ch.link(pool.affine_select(out=view, in_=view, compare_op=op, fill=fill, base=base,
                                           pattern=pattern, channel_multiplier=cm))

            ch.link(pool.memset(ident[:, :], 0.0))
            keep(ident, ident[:, :], [[-1, P]], 0, 1, ALU.not_equal, 1.0)
            pool.memset(neghalf[:, :], -0.5).then_inc(S("ident_ok"), 1)
            ch.link(pool.memset(head_ones[:, :], 0.0))
            ch.link(pool.memset(head_ones[0:64, 0:64], 1.0))
            ch.link(pool.memset(head_ones[64:128, 64:128], 1.0))
            ch.link(pool.tensor_copy(mask_su[:, :], head_ones[:, :]))
            ch.link(pool.tensor_copy(mask_iu[:, :], head_ones[:, :]))
            keep(mask_su, mask_su[:, :], [[1, P]], 0, -1, ALU.is_gt)
            keep(mask_iu, mask_iu[:, :], [[1, P]], 0, -1, ALU.is_ge)
            ch.link(pool.memset(lvl[:, :, :], 1.0))
            for l in range(6):
                b = 1 << l
                v = lvl[:, l, :].rearrange("p (q h r) -> p q h r", h=2, r=b)
                keep(lvl, v, [[-2 * b, P // (2 * b)], [-1000, 2], [0, b]], -b, 1, ALU.is_ge)
                keep(lvl, v, [[2 * b, P // (2 * b)], [0, 2], [0, b]], 2 * b - 1, -1, ALU.is_ge)
            ch.link(pool.memset(lvl0T[:, :], 1.0))
            keep(lvl0T, lvl0T[:, :].rearrange("p (q h) -> p q h", h=2), [[-2, 64], [-1000, 2]], 1000, 1, ALU.is_equal)
            ch.link(pool.iota(dist[:, :], [[1, 512]], base=-384, channel_multiplier=-1,
                              allow_small_or_imprecise_dtypes=True))
            keep(dist, dist[:, :], [[-1, 512]], 384, 1, ALU.is_ge, -1.0e30)
            ch.link(pool.memset(SCM[:, :], 1.0))
            pool.memset(SCM[:, :].rearrange("p (c t) -> p c t", t=CH + 1)[:, :, 0:1], 0.0)
            pool.memset(onesf[:, :], 1.0)
            pool.memset(ones_b[:, :], 1.0)
            pool.iota(iota32[:, :], [[1, NE]], base=0, channel_multiplier=0, allow_small_or_imprecise_dtypes=True)
            pool.iota(iotaB[:, :], [[1, NBT]], base=0, channel_multiplier=0, allow_small_or_imprecise_dtypes=True)
            pool.iota(iotaR[:, :], [[1, P]], base=0, channel_multiplier=0, allow_small_or_imprecise_dtypes=True)
            pool.iota(pair_ids[:, 0, :], [[0, 16]], base=0, channel_multiplier=4, allow_small_or_imprecise_dtypes=True)
            pool.iota(pair_ids[:, 1, :], [[512, 4], [0, 4]], base=0, channel_multiplier=0,
                      allow_small_or_imprecise_dtypes=True)
            ch.link(pool.iota(pair_ids[:, 2, :], [[0, 4], [1, 4]], base=1, channel_multiplier=0,
                              allow_small_or_imprecise_dtypes=True))
            for q in range(4):
                ch.link(pool.iota(lane32[32 * q:32 * q + 32, :], [[0, 1]], base=0, channel_multiplier=1,
                                  allow_small_or_imprecise_dtypes=True))
            ch.link(pool.memset(triu[:, :], 1.0))
            keep(triu, triu[:, :], [[1, P]], 0, -1, ALU.is_gt)
            pool.sem_inc(S("consts_ok"), 1)

            pool.wait_ge(S("ms_ok"), 1)
            pool.tensor_tensor(rms[:, 0:4], ss[:, 0:4], neghalf[:, :].to_broadcast([P, 4]), ALU.pow)\
                .then_inc(S("rms_ok"), 1)

            bias_src = [t_in[k][0] for k in ("moe_b_gate", "moe_b_up", "moe_b_down")]
            for w in range(3):
                for q in range(3):
                    pool.dma_start(bias_raw[32 * q:32 * q + 32, :], bias_src[w]).then_inc(S("bias_in"), 16)
                pool.wait_ge(S("bias_in"), 48 * (w + 1))
                for q in range(3):
                    lo, n = 32 * q, 96 - 32 * q
                    for r in range(lo, 96, 32):
                        ch.link(pool.tensor_copy(biasb[r:r + 32, w, :], bias_raw[r:r + 32, :]))
                    if q < 2:
                        for r in range(lo + 32, 96, 32):
                            ch.link(pool.tensor_tensor(bias_raw[r:r + 32, :], bias_raw[r:r + 32, :],
                                                       biasb[r:r + 32, w, :], ALU.subtract))

            pool.wait_ge(S("zero_columns"), 1)
            for i in range(14):
                rows = (64, 96)[i - 12] if i >= 12 else P
                pool.wait_ge(S("unshifted_ok"), i + 1)
                if i >= 2:
                    pool.wait_ge(S("shifted_ok"), i - 1)
                pool.tensor_tensor(DF[0:rows, i % 2, :], XR[0:rows, i % 2, 0:512], XR[0:rows, i % 2, 1:513],
                                   ALU.subtract).then_inc(S("diff_ok"), 1)

            for qt in range(TT):
                pool.wait_ge(S("att_ms"), qt + 1)
                pool.tensor_tensor(hrs[:, qt, :], hss[:, qt, :], neghalf[:, :].to_broadcast([P, 8]), ALU.pow)\
                    .then_inc(S("att_rms"), 1)

            pool.wait_ge(S("att_done"), 1)
            pool.memset(SIG[:, :, :, 0:1], 0.0).then_inc(S("sig_zero"), 1)
            for h in range(HP):
                pool.wait_ge(S("sig_ok"), h + 1)
                pool.wait_ge(S("kk_raw"), h + 1)
                ch.link(pool.tensor_scalar(T1[:, h % 2, :], AV[:, h, :], par[:, KA_ + h:KA_ + h + 1],
                                           one_m_ka[:, h:h + 1], ALU.mult, ALU.add))
                ch.link(pool.tensor_tensor(KX[:, h, :], KX[:, h, :], T1[:, h % 2, :], ALU.mult))
            pool.sem_inc(S("keys_ok"), 1)
            pool.wait_ge(S("prep_done"), 1)
            pool.memset(ST[:, :, :], 0.0).then_inc(S("state_written"), 1)
            RKP = par[:, RK_:RK_ + HP]
            lc = Chain(pool, "pool_tile_chain")
            with pool.Fori(0, TT) as tt:
                lc.base, lc.n = tt * 1, 0
                pool.wait_ge(S("exp_ok"), tt * 2 + 2)
                pool.tensor_tensor(KSt[:, :, :].rearrange("p h (c t) -> p h c t", t=CH), tile_chunks(KX[:, :, :], tt),
                                   EI[:, :, :, :], ALU.mult)
                pool.tensor_tensor(RSt[:, :, :].rearrange("p h (c t) -> p h c t", t=CH), tile_chunks(RX[:, :, :], tt),
                                   E01[:, :, :, 1:CH + 1], ALU.mult).then_inc(S("kr_tile"), 1)
                lc.link(pool.tensor_tensor(BP[:, :, :], tiles(RX[:, :, :], tt), tiles(KX[:, :, :], tt), ALU.mult))
                pool.tensor_tensor(BP[:, :, :], BP[:, :, :], bc(RKP, [P, HP, P], 2), ALU.mult)\
                    .then_inc(S("bonus_prod"), 1)
                pool.wait_ge(S("map_masked"), tt + 1)
                for c in range(2):
                    ins = pool.tensor_tensor(MTm[:, c], MTm[:, c], eye4, ALU.add)
                ins.then_inc(S("map_ok"), 1)

            pool.wait_ge(S("ms_ok"), 2)
            pool.tensor_tensor(rms[:, 4:8], ss[:, 4:8], neghalf[:, :].to_broadcast([P, 4]), ALU.pow)\
                .then_inc(S("rms_ok"), 1)

            pool.wait_ge(S("tables_ok"), 1)
            nb = pool.value_load(n_blk[0:1, 0:1], min_val=16, max_val=NB - 1)
            last_blk = pool.value_load(n_blk[0:1, 1:2], min_val=15, max_val=NB - 2)
            pool.wait_ge(S("xn2_stored"), 16 * TT)
            pool.memset(XB[:, :, :], 0.0).then_inc(S("xb_zero"), 1)
            pool.wait_ge(S("xb_zero"), 1)

            last_x, last_y = pool.to_reg(SEQ - 1), pool.to_reg(SEQ * TOPK - 1)
            ic = Chain(pool, "index_chain")

            def gather(j, q, links):
                ic.base, ic.n = links, 0
                ic.link(pool.tensor_copy(now_x[q][:, :], idx_x[:, ds(j, 1)]))
                pool.sem_inc(S("index_ready"), 1)
                pool.indirect_dma_start(
                    out=XB[:, q, :], out_offset=None, in_=xn2_d,
                    in_offset=bass.IndirectOffsetOnAxis(ap=now_x[q][:, :].bitcast(U32), axis=0),
                    bounds_check=last_x, oob_is_err=False).then_inc(S(f"xb_in{q}"), 16)

            def scatter(j, links):
                if not (isinstance(j, int) and j == 0):
                    pool.wait_ge(S("y_stored"), j * 16)
                ic.base, ic.n = links, 0
                ic.link(pool.tensor_copy(now_y[:, :], idx_y[:, ds(j, 1)]))
                pool.sem_inc(S("index_ready"), 1)
                pool.indirect_dma_start(
                    out=y_d, out_offset=bass.IndirectOffsetOnAxis(ap=now_y[:, :].bitcast(U32), axis=0),
                    in_=YB[:, :], in_offset=None,
                    bounds_check=last_y, oob_is_err=False).then_inc(S("y_stored"), 16)

            def select(j):
                pool.tensor_copy(bsel[:, :], expsel[:, ds(j, 1)].to_broadcast([96, P])).then_inc(S("bias_sel"), 1)

            gather(0, 0, 0)
            gather(1, 1, 1)
            select(0)

            def block_pool(i, q, prev):
                pool.wait_ge(S("up_down_bias"), i + 1)
                pool.wait_ge(S("xT_ps"), i + 1)
                select(i + 1)
                gather(i + 2, q, 2 if prev is None else i * 2 + 1)
                if prev is not None:
                    pool.wait_ge(S("y_act"), i)
                    pool.wait_ge(S("y_dve"), i)
                    scatter(prev, i * 2 + 2)

            block_pool(0, 0, None)
            block_pool(1, 1, 0)
            with pool.Fori(0, (NB - 2) // 2) as it:
                for q in range(2):
                    i = it * 2 + (2 + q)
                    with pool.If(i < nb):
                        block_pool(i, q, it * 2 + (1 + q))
            pool.wait_ge(S("y_act"), nb)
            pool.wait_ge(S("y_dve"), nb)
            scatter(last_blk, nb * 2 + 1)
            pool.wait_ge(S("y_stored"), nb * 16)
            pool.wait_ge(S("xb_in0"), (nb + 3) // 2 * 16)
            pool.wait_ge(S("xb_in1"), (nb + 2) // 2 * 16)
            for tt in range(TT):
                pool.wait_ge(S("ms_final"), tt + 1)
                pool.tensor_tensor(rms[:, 8 + tt:9 + tt], ss[:, 8 + tt:9 + tt], neghalf[:, :], ALU.pow)\
                    .then_inc(S("rms_final"), 1)

        def xT_hi(act, j, q):
            act.wait_ge(S("xT_ps"), j + 1)
            for b in range(2):
                ins = act.activation(xbh[q][:, 4 * b:4 * b + 4, :].rearrange("p k t -> p (k t)"), bank[6 + b], ACT.Copy)
            ins.then_inc(S("xT_hi"), 1)

        def y_act(act, i, prev):
            act.wait_ge(w_used, i * PER + (MOE0 + 8))
            if not (isinstance(prev, int) and prev == 0):
                act.wait_ge(S("y_stored"), prev * 16)
            act.activation(YB[:, 0:512], bank[4], ACT.Copy).then_inc(S("y_act"), 1)

        def block_act(act, i, q, prev):
            base = MOE0 + 8 + i * PER

            def hi(k):
                xring.make_hi(act, base + k, 8 + k, i * (PER // NRAW2) + (8 + k) // NRAW2)

            for k in range(2):
                hi(k)
            act.wait_ge(S("gate_ok"), i + 1)
            act.activation(SG[:, :], GT[:, :], ACT.Sigmoid, scale=ALPHA).then_inc(S("sigmoid_ok"), 1)
            for k in range(2, 4):
                hi(k)
            if prev is not None:
                y_act(act, i, prev)
            for k in range(4, 8):
                hi(k)
            xT_hi(act, i + 1, 1 - q)
            for k in range(8, 17):
                hi(k)
            act.wait_ge(S("hT_ps"), i + 1)
            for b in range(2):
                ins = act.activation(hbh[:, 4 * b:4 * b + 4, :].rearrange("p k t -> p (k t)"), bank[6 + b], ACT.Copy)
            ins.then_inc(S("hT_hi"), 1)
            for k in range(17, 24):
                hi(k)

        @block.scalar
        def _(act):
            act.dma_start(g_mix[:, :], t_in["norm_mix_g"][0].rearrange("(p k) -> p k", k=KT)).then_inc(S("params_in"), 16)
            act.dma_start(w2a2[0:32, :], t_in["rwkv_w2"][0]).then_inc(S("params_in"), 16)
            act.dma_start(w2a2[32:64, :], t_in["rwkv_a2"][0]).then_inc(S("params_in"), 16)
            act.dma_start(g2[:, :], t_in["rwkv_g2"][0]).then_inc(S("params_in"), 16)
            act.dma_start(w_rout[:, :, :], t_in["w_router"][0].rearrange("(p k) e -> p k e", k=KT))\
                .then_inc(S("params_in"), 16)
            act.dma_start(b_rout[:, :], t_in["b_router"][0].partition_broadcast(P)).then_inc(S("params_in"), 16)
            act.wait_ge(S("param_rows_zero"), 1)
            mu = t_in["rwkv_mu"][0]
            act.dma_start(par_rows[MU:MU + 12, :], mu[0:1536].rearrange("(r c) -> r c", c=P)).then_inc(S("params_in"), 16)
            act.dma_start(par_rows[MU + 12:MU + 13, 0:64], mu[1536:1600].unsqueeze(0)).then_inc(S("params_in"), 16)
            act.dma_start(par_rows[MU + 13:MU + 14, 0:96], mu[1600:1696].unsqueeze(0)).then_inc(S("params_in"), 16)
            for row, name in ((W0, "rwkv_w0"), (A0, "rwkv_a0"), (KK_, "rwkv_k_k"), (KA_, "rwkv_k_a"),
                              (LNG, "rwkv_ln_g"), (LNB, "rwkv_ln_b"), (ATG, "attn_norm_g")):
                act.dma_start(par_rows[row:row + 4, :], t_in[name][0].rearrange("(r c) -> r c", c=P))\
                    .then_inc(S("params_in"), 16)
            act.dma_start(par_rows[RK_:RK_ + 4, :], t_in["rwkv_r_k"][0].rearrange("(r a) c -> r (a c)", a=2))\
                .then_inc(S("params_in"), 16)

            act.wait_ge(S("x_in"), 64)
            for tt in range(TT):
                ins = act.activation(pair[tt][:, :], H[:, tt, :], ACT.Square, accum_out=ss[:, tt:tt + 1])
            ins.then_inc(S("squares_ok"), 1)
            hi_range(act, 0, 4)
            act.wait_ge(S("params_in"), 16 * NPAR)
            act.wait_ge(S("xT_first"), TT)
            for k in range(KT):
                act.activation(xnh[:, k, :], bank[k], ACT.Copy, scale=g_mix[:, k:k + 1]).then_inc(S("xnh_ok"), 1)

            for g in range(7):
                b0 = (g % 2) * 4
                hi_range(act, 4 * g + 4, min(4 * g + 8, IN_CH + NHL))
                act.wait_ge(w_used, min(4 * g + 4, IN_CH))
                if g == 0:
                    for c in range(4):
                        ins = act.activation(QT[:, c, :], bank[b0 + c], ACT.Copy, scale=HD ** -0.5)
                    ins.then_inc(S("qv_out"), 1)
                elif g == 2:
                    for c in range(4):
                        ins = act.activation(VA[:, c, :], bank[b0 + c], ACT.Copy)
                    ins.then_inc(S("qv_out"), 1)
                elif g >= 3:
                    for c in range(4 if g < 6 else 2):
                        i = 4 * (g - 3) + c
                        rows = P if g < 6 else (64, 96)[c]
                        if i >= 2:
                            act.wait_ge(S("shifted_ok"), i - 1)
                        act.activation(XR[0:rows, i % 2, 1:513], bank[b0 + c][0:rows, :], ACT.Copy)\
                            .then_inc(S("unshifted_ok"), 1)

            for u in range(17):
                if u < 16:
                    nk, z = (u // 4 + 1) * P, u % 2
                    act.wait_ge(S("scores_ok"), u + 1)
                    if u >= 2:
                        act.wait_ge(S("probsT_ps"), u - 1)
                    for j in range(2):
                        ins = act.activation(PR[:, z, j, 0:nk], SC[:, z, j, 0:nk], ACT.Exp,
                                             bias=nmax[:, 2 * u + j:2 * u + j + 1],
                                             accum_out=rsum[:, 2 * u + j:2 * u + j + 1])
                    ins.then_inc(S("probs_ok"), 1)
                if u >= 1:
                    v = u - 1
                    nk = (v // 4 + 1) * P
                    act.wait_ge(S("probsT_ps"), v + 1)
                    if v >= 2:
                        act.wait_ge(S("att_pv"), v - 1)
                    act.activation(PRT[:, v % 2, :, 0:nk], pair[2][:, :].rearrange("p (j k) -> p j k", j=2)[:, :, 0:nk],
                                   ACT.Copy).then_inc(S("probsT_ok"), 1)

            act.wait_ge(S("att_done"), 1)
            act.activation(TL[:, :], XL[0:32, 0, :], ACT.Tanh)
            act.activation(XL[0:96, 1, :], XL[0:96, 1, :], ACT.Sigmoid).then_inc(S("lora_in"), 1)
            for h in range(HP):
                act.wait_ge(S("lora_ps"), h + 1)
                act.activation(SIG[:, h, :, 1:CH + 1], bank[h].rearrange("p (c t) -> p c t", t=CH), ACT.Sigmoid,
                               bias=par[:, W0 + h:W0 + h + 1])
                act.activation(AV[:, h, :], bank[4 + h], ACT.Sigmoid, bias=par[:, A0 + h:A0 + h + 1])\
                    .then_inc(S("sig_ok"), 1)
            for h in range(HP):
                act.wait_ge(S("kk_raw"), h + 1)
                if h >= 2:
                    act.wait_ge(S("kk_ss_ps"), h - 1)
                act.activation(T4[:, h % 2, :], KKN[:, h, :], ACT.Square).then_inc(S("kk_sq"), 1)
            for h in range(HP):
                act.wait_ge(S("kk_ss_read"), h + 1)
                if h >= 2:
                    act.wait_ge(S("kk_normed"), h - 1)
                act.activation(T3[:, h % 2, :], T2[:, h % 2, :], ACT.Sqrt).then_inc(S("kk_root"), 1)
            act.wait_ge(S("prep_done"), 1)
            with act.Fori(0, TT) as tt:
                act.wait_ge(S("state_written"), tt * 2 + 1)
                cs = CS[:, :, ds(tt * 2, 2), :]
                act.activation(E01[:, :, :, :], cs, ACT.Exp, scale=-DECAY).then_inc(S("exp_ok"), 1)
                act.activation(EI[:, :, :, :], cs[:, :, :, 1:CH + 1], ACT.Exp, scale=DECAY).then_inc(S("exp_ok"), 1)
                act.activation(VSt[:, :, :], tiles(VX[:, :, :], tt), ACT.Copy).then_inc(S("v_tile"), 1)
                act.wait_ge(S("rows_ps"), tt + 1)
                act.activation(Bt[:, :], bank[1], ACT.Copy)
                act.activation(Kt[:, :], bank[2], ACT.Copy)
                act.activation(Vt[:, :], bank[3], ACT.Copy).then_inc(S("bkv_rows"), 1)
                for j in range(2):
                    act.wait_ge(S("AT_ps"), tt + 1)
                    ins = act.activation(AsT[:, j].rearrange("p h t -> p (h t)"), bank[4 + j], ACT.Copy)
                ins.then_inc(S("AT_ok"), 1)
                act.wait_ge(S("z0_ps"), tt + 1)
                act.activation(AZ[:, :, 1, :], bank[6].rearrange("p (h d) -> p h d", d=CH), ACT.Copy)\
                    .then_inc(S("z0_rows"), 1)
                act.wait_ge(S("uz_ps"), tt + 1)
                uz = UZ[:, :, :, :].rearrange("p c (h j) d -> p j h c d", j=2)
                for j in range(2):
                    ins = act.activation(uz[:, j], bank[6 + j].rearrange("p (h c d) -> p h c d", h=HP, c=2), ACT.Copy)
                ins.then_inc(S("uz_rows"), 1)
                act.wait_ge(S("out_ps"), tt + 1)
                act.activation(tiles(RX[:, :, :], tt), bank[5].rearrange("p (h t) -> p h t", t=P), ACT.Copy)\
                    .then_inc(S("rwkv_out"), 1)

            act.wait_ge(S("state_written"), 2 * TT + 1)
            for h in range(HP):
                act.wait_ge(S("gate_ps"), h + 1)
                act.activation(G[:, h, :], bank[h], ACT.Copy).then_inc(S("gate_out"), 1)
            for c in range(4):
                act.activation(mxh[:, c, :], MA[:, c, :], ACT.Copy).then_inc(S("mix_hi_ok"), 1)
            for h in range(HP + 1):
                if h < HP:
                    act.wait_ge(S("gn_centered"), h + 1)
                    if h >= 2:
                        act.wait_ge(S("gn_normed"), h - 1)
                    act.activation(U2[:, h % 2, :], U1[:, h % 2, :], ACT.Square).then_inc(S("gn_sq"), 1)
                if h >= 1:
                    act.wait_ge(S("gn_normed"), h)
                    act.activation(mxh[:, 3 + h, :], U1[:, (h - 1) % 2, :], ACT.Copy).then_inc(S("mix_hi_ok"), 1)
                if h < HP:
                    act.wait_ge(S("gn_var"), h + 1)
                    act.activation(U3[:, h % 2, :], U2[:, h % 2, :], ACT.Sqrt).then_inc(S("gn_root"), 1)
            hi_range(act, IN_CH + NHL, MOE0)
            act.wait_ge(S("mix_added"), 8)
            for tt in range(TT):
                ins = act.activation(pair[tt][:, :], H[:, tt, :], ACT.Square, accum_out=ss[:, 4 + tt:5 + tt])
            ins.then_inc(S("squares_ok"), 1)
            act.wait_ge(S("x2T_ps"), TT)
            for k in range(0, KT, 2):
                act.activation(X2T[:, k, :], bank[k], ACT.Copy).then_inc(S("x2T_act"), 1)
            act.wait_ge(S("top_ok"), 1)
            for tt in range(TT):
                ins = act.activation(gates[:, tt, :], top8[:, tt, 0:4], ACT.Exp, bias=ntop[:, tt:tt + 1],
                                     accum_out=gsum[:, tt:tt + 1])
            ins.then_inc(S("gate_exp"), 1)

            act.wait_ge(S("tables_ok"), 1)
            nb = act.value_load(n_blk[0:1, 0:1], min_val=16, max_val=NB - 1)
            last_blk = act.value_load(n_blk[0:1, 1:2], min_val=15, max_val=NB - 2)
            for c in range(8):
                if c == 4:
                    xT_hi(act, 0, 0)
                xring.make_hi(act, MOE0 + c, c, c // NRAW2)
            block_act(act, 0, 0, None)
            block_act(act, 1, 1, 0)
            with act.Fori(0, (NB - 2) // 2) as it:
                for q in range(2):
                    i = it * 2 + (2 + q)
                    with act.If(i < nb):
                        block_act(act, i, q, it * 2 + (1 + q))
            y_act(act, nb, last_blk)
            for tt in range(TT):
                act.wait_ge(S("combined"), tt + 1)
                act.activation(pair[tt][:, :], H[:, tt, :], ACT.Square,
                               accum_out=ss[:, 8 + tt:9 + tt]).then_inc(S("squares_final"), 1)


        def xT_lo(dve, j, q):
            dve.wait_ge(S("xT_hi"), j + 1)
            for b in range(2):
                ins = dve.tensor_tensor(xbl[q][:, 4 * b:4 * b + 4, :].rearrange("p k t -> p (k t)"), bank[6 + b],
                                        xbh[q][:, 4 * b:4 * b + 4, :].rearrange("p k t -> p (k t)").bitcast(F32),
                                        ALU.subtract)
            ins.then_inc(S("xT_ok"), 1)

        def gate_part(dve, j):
            if isinstance(j, int) and j == 0:
                dve.wait_ge(w_used, MOE0 + 8)
            else:
                dve.wait_ge(w_used, j * PER + MOE0)
                dve.wait_ge(S("h_ok"), j)
            dve.tensor_scalar(GT[:, :], pair[0][:, :], LIMIT, None, ALU.min).then_inc(S("gate_ok"), 1)

        def y_dve(dve, i, prev):
            dve.wait_ge(w_used, i * PER + (MOE0 + 8))
            if not (isinstance(prev, int) and prev == 0):
                dve.wait_ge(S("y_stored"), prev * 16)
            dve.tensor_copy(YB[:, 512:1024], bank[5]).then_inc(S("y_dve"), 1)

        def block_dve(dve, i, q, prev):
            base = MOE0 + 8 + i * PER

            def lo(k):
                xring.make_lo(dve, base + k, 8 + k)

            for k in range(3):
                lo(k)
            dve.wait_ge(S("sigmoid_ok"), i + 1)
            dve.tensor_tensor(GT[:, :], GT[:, :], SG[:, :], ALU.mult).then_inc(S("glu_ok"), 1)
            lo(3)
            if prev is not None:
                y_dve(dve, i, prev)
            for k in range(4, 8):
                lo(k)
            xT_lo(dve, i + 1, 1 - q)
            for k in range(8, 12):
                lo(k)
            dve.wait_ge(w_used, base + 8)
            dve.tensor_scalar(UP[:, :], pair[1][:, :], LIMIT, -LIMIT, ALU.min, ALU.max).then_inc(S("up_ok"), 1)
            dve.wait_ge(S("up_ok"), i + 1)
            dve.wait_ge(S("glu_ok"), i + 1)
            dve.scalar_tensor_tensor(HB[:, :], UP[:, :], 1.0, GT[:, :], ALU.add, ALU.mult).then_inc(S("h_ok"), 1)
            for k in range(12, 17):
                lo(k)
            dve.wait_ge(S("hT_hi"), i + 1)
            for b in range(2):
                ins = dve.tensor_tensor(hbl[:, 4 * b:4 * b + 4, :].rearrange("p k t -> p (k t)"), bank[6 + b],
                                        hbh[:, 4 * b:4 * b + 4, :].rearrange("p k t -> p (k t)").bitcast(F32),
                                        ALU.subtract)
            ins.then_inc(S("hT_ok"), 1)
            for k in range(17, 20):
                lo(k)
            gate_part(dve, i + 1)
            for k in range(20, 24):
                lo(k)

        @block.vector
        def _(dve):
            ch = Chain(dve, "dve_chain")
            dve.wait_ge(S("param_ps"), 1)
            ch.link(dve.tensor_copy(par[:, :], bank[7][:, 0:48]))
            dve.tensor_scalar(one_m_ka[:, :], par[:, KA_:KA_ + 4], -1.0, 1.0, ALU.mult, ALU.add).then_inc(S("params_ok"), 1)

            dve.wait_ge(S("squares_ok"), 1)
            dve.tensor_scalar(ss[:, 0:4], ss[:, 0:4], 1.0 / D, EPS, ALU.mult, ALU.add).then_inc(S("ms_ok"), 1)
            lo_range(dve, 0, 4)
            dve.wait_ge(S("rms_ok"), 1)
            for tt in range(TT):
                if tt >= 2:
                    dve.wait_ge(S("xT_first"), tt - 1)
                dve.tensor_scalar(xs[:, tt % 2, :], H[:, tt, :], rms[:, tt:tt + 1], None, ALU.mult).then_inc(S("xs_ok"), 1)
            for k in range(KT):
                dve.wait_ge(S("xnh_ok"), k + 1)
                dve.scalar_tensor_tensor(xnl[:, k, :], bank[k], g_mix[:, k:k + 1], xnh[:, k, :].bitcast(F32),
                                         ALU.mult, ALU.subtract).then_inc(S("xnl_ok"), 1)

            dsts = [RX, KX, VX]
            for g in range(7):
                b0 = (g % 2) * 4
                lo_range(dve, 4 * g + 4, min(4 * g + 8, IN_CH + NHL))
                if g == 1:
                    dve.wait_ge(w_used, 8)
                    for c in range(4):
                        ins = dve.tensor_copy(KTT[:, c, :], bank[b0 + c])
                    ins.then_inc(S("group1_out"), 1)
                elif g >= 3:
                    for c in range(4 if g < 6 else 2):
                        i = 4 * (g - 3) + c
                        rows = P if g < 6 else (64, 96)[c]
                        dst = dsts[g - 3][:, c, :] if g < 6 else XL[0:rows, c, :]
                        dve.wait_ge(S("diff_ok"), i + 1)
                        dve.scalar_tensor_tensor(dst, DF[0:rows, i % 2, :], par[0:rows, MU + i:MU + i + 1],
                                                 XR[0:rows, i % 2, 1:513], ALU.mult, ALU.add)\
                            .then_inc(S("shifted_ok"), 1)

            def finish_queries(qt):
                b = bank[6 + qt % 2].rearrange("p (h d) -> p h d", d=HD)
                dve.wait_ge(S("att_pv"), 4 * (qt + 1))
                if qt:
                    dve.wait_ge(S("attT_ps"), qt)
                ch.link(dve.reciprocal(rinv[:, 8 * qt:8 * qt + 8], rsum[:, 8 * qt:8 * qt + 8]))
                ch.link(dve.tensor_tensor(ON[:, :, :], b, bc(rinv[:, 8 * qt:8 * qt + 8], [P, 8, HD], 2), ALU.mult))
                ch.link(dve.tensor_tensor(OSQ[:, :, :], ON[:, :, :], ON[:, :, :], ALU.mult))
                ch.link(dve.reduce_sum(hss[:, qt, :], OSQ[:, :, :], AXX))
                dve.tensor_scalar(hss[:, qt, :], hss[:, qt, :], 1.0 / HD, EPS, ALU.mult, ALU.add).then_inc(S("att_ms"), 1)
                dve.wait_ge(S("att_rms"), qt + 1)
                dve.tensor_tensor(ON[:, :, :], ON[:, :, :], bc(hrs[:, qt, :], [P, 8, HD], 2), ALU.mult)\
                    .then_inc(S("att_on"), 1)

            def gain(qt):
                dve.wait_ge(S("attT_ps"), qt + 1)
                return dve.tensor_tensor(MA[:, :, qt * P:(qt + 1) * P], bank[4].rearrange("p (c t) -> p c t", t=P),
                                         bc(par[:, ATG:ATG + 4], [P, 4, P], 2), ALU.mult)

            for u in range(16):
                nk, z = (u // 4 + 1) * P, u % 2
                dve.wait_ge(S("scores_ps"), u + 1)
                if u >= 2:
                    dve.wait_ge(S("probs_ok"), u - 1)
                for j in range(2):
                    ins = dve.scalar_tensor_tensor(SC[:, z, j, 0:nk], dist[:, 512 - nk:512], 2.0 ** -(2 * (u % 4) + j + 1),
                                                   bank[2 * z + j][:, 0:nk], ALU.mult, ALU.add)
                ch.link(ins)
                dve.reduce_max(nmax[:, 2 * u:2 * u + 2], SC[:, z, :, 0:nk], AXX, negate=True).then_inc(S("scores_ok"), 1)
                if u % 4 == 3 and u > 4:
                    finish_queries(u // 4 - 1)
                    gain(u // 4 - 1).then_inc(S("att_gained"), 1)
            finish_queries(3)
            gain(3).then_inc(S("att_gained"), 1)
            dve.wait_ge(S("att_gained"), 4)
            dve.wait_ge(S("probsT_ok"), 16)
            dve.sem_inc(S("att_done"), 1)

            def inverse_root(y, x, tmp):
                ch.link(dve.reciprocal(y, y))
                ch.link(dve.tensor_tensor(tmp, y, y, ALU.mult))
                ch.link(dve.scalar_tensor_tensor(tmp, tmp, -0.5, x, ALU.mult, ALU.mult))
                ch.link(dve.scalar_tensor_tensor(y, tmp, 1.5, y, ALU.add, ALU.mult))

            dve.wait_ge(S("sig_zero"), 1)
            for h in range(HP):
                dve.tensor_scalar(KKN[:, h, :], KX[:, h, :], par[:, KK_ + h:KK_ + h + 1], None, ALU.mult)\
                    .then_inc(S("kk_raw"), 1)
            for h in range(HP):
                dve.wait_ge(S("sig_ok"), h + 1)
                dve.tensor_tensor_scan(CS[:, h, :, :].rearrange("p c t -> p (c t)"), SCM[:, :],
                                       SIG[:, h, :, :].rearrange("p c t -> p (c t)"), 0.0, ALU.mult, ALU.add)
            for h in range(HP + 1):
                if h < HP:
                    dve.wait_ge(S("kk_ss_ps"), h + 1)
                    dve.tensor_scalar(T2[:, h % 2, :], bank[h], 1e-24, None, ALU.max).then_inc(S("kk_ss_read"), 1)
                if h >= 1:
                    g = h - 1
                    dve.wait_ge(S("kk_root"), g + 1)
                    inverse_root(T3[:, g % 2, :], T2[:, g % 2, :], T5[:, :])
                    ch.link(dve.scalar_tensor_tensor(KKN[:, g, :], KKN[:, g, :], -1.0, T3[:, g % 2, :], ALU.mult, ALU.mult))
                    dve.scalar_tensor_tensor(BV[:, g, :], KKN[:, g, :], -1.0, AV[:, g, :], ALU.mult, ALU.mult)\
                        .then_inc(S("kk_normed"), 1)
            dve.wait_ge(S("kk_normed"), HP)
            dve.wait_ge(S("keys_ok"), 1)
            dve.sem_inc(S("prep_done"), 1)

            def m4(m):
                return bc(m, [P, HP, P], 1)

            def bk(b):
                return bank[b].rearrange("p (h t) -> p h t", t=P)

            lc = Chain(dve, "dve_tile_chain")
            DVE_LINKS = 4
            with dve.Fori(0, TT) as tt:
                lc.base, lc.n = tt * DVE_LINKS, 0
                dve.wait_ge(S("exp_ok"), tt * 2 + 2)
                dve.tensor_tensor(ASt[:, :, :].rearrange("p h (c t) -> p h c t", t=CH), tile_chunks(KKN[:, :, :], tt),
                                  E01[:, :, :, 0:CH], ALU.mult)
                dve.tensor_tensor(BSt[:, :, :].rearrange("p h (c t) -> p h c t", t=CH), tile_chunks(BV[:, :, :], tt),
                                  EI[:, :, :, :], ALU.mult).then_inc(S("ab_tile"), 1)
                dve.wait_ge(S("rows_ps"), tt + 1)
                dve.tensor_copy(AZ[:, :, 0, :], bank[0].rearrange("p (h d) -> p h d", d=CH)).then_inc(S("a_rows"), 1)
                dve.wait_ge(S("AT_ps"), tt + 1)
                for j in range(2):
                    dve.tensor_tensor(Xi[:, j], bk(6 + j), m4(lvl[:, 0, :]), ALU.mult)
                dve.wait_ge(S("AT_ok"), tt + 1)
                for j in range(2):
                    ins = dve.tensor_tensor(XiT[:, j], bk(4 + j), m4(lvl0T[:, :]), ALU.mult)
                lc.link(ins)
                for j in range(2):
                    dve.tensor_tensor(XiT[:, j], XiT[:, j], eye4, ALU.add)
                    dve.tensor_tensor(Xi[:, j], Xi[:, j], eye4, ALU.add).then_inc(S("inv_ok"), 1)
                dve.wait_ge(S("TK_ps"), tt + 1)
                for j in range(2):
                    ins = dve.tensor_tensor(TKm[:, j], bk(j), m4(mask_su[:, :]), ALU.mult)
                ins.then_inc(S("TK_ok"), 1)
                for j in range(2):
                    ins = dve.tensor_tensor(RBm[:, j], bk(2 + j), m4(mask_iu[:, :]), ALU.mult)
                ins.then_inc(S("RB_ok"), 1)
                dve.wait_ge(S("RK_ps"), tt + 1)
                for j in range(2):
                    ins = dve.tensor_tensor(RKm[:, j], bk(4 + j), m4(mask_iu[:, :]), ALU.mult)
                ins.then_inc(S("RK_ok"), 1)
                vt = tiles(VX[:, :, :], tt)
                dve.wait_ge(S("v_tile"), tt + 1)
                dve.wait_ge(S("bonus_ps"), tt + 1)
                dve.tensor_tensor(vt, bk(6), vt, ALU.mult).then_inc(S("bonus_ok"), 1)
                for l in range(1, 6):
                    for j in range(2):
                        dve.wait_ge(S("step_ps"), tt * 10 + (2 * (l - 1) + j + 1))
                        dve.tensor_tensor(Pm[:, j], bk(j), m4(lvl[:, l, :]), ALU.mult).then_inc(S("step_ok"), 1)
                    for j in range(2):
                        dve.wait_ge(S("inv_ps"), tt * 10 + (2 * (l - 1) + j + 1))
                        if l < 5:
                            dve.tensor_tensor(Xi[:, j], Xi[:, j], bk(2 + j), ALU.add)
                        dve.tensor_tensor(XiT[:, j], XiT[:, j], bk(4 + j), ALU.add).then_inc(S("inv_ok"), 1)
                dve.wait_ge(S("map_ps"), tt + 1)
                for c in range(2):
                    ins = dve.tensor_tensor(MTm[:, c], bk(1 + c), m4(head_ones[:, :]), ALU.mult)
                ins.then_inc(S("map_masked"), 1)
                dve.wait_ge(S("r2_ps"), tt + 1)
                dve.tensor_tensor(R2[:, :, :], bk(0), RSt[:, :, :], ALU.add).then_inc(S("r2_ok"), 1)
                dve.wait_ge(S("add_ps"), tt + 1)
                for c in range(2):
                    ins = dve.tensor_tensor(NN[:, c], bk(3 + c), m4(head_ones[:, :]), ALU.mult)
                lc.link(ins)
                for c in range(2):
                    dve.wait_ge(S("chain_ps"), tt * 2 + (c + 1))
                    lc.link(dve.tensor_tensor(SN[:, :, :], bk(6 + c), NN[:, c], ALU.add))
                    dve.tensor_tensor(ST[:, :, :], SN[:, :, :],
                                      E01[:, :, c, CH:CH + 1].to_broadcast([P, HP, P]), ALU.mult)\
                        .then_inc(S("state_written"), 1)
                assert lc.n == DVE_LINKS

            for c in range(4):
                dve.wait_ge(S("mix_hi_ok"), c + 1)
                dve.tensor_tensor(mxl[:, c, :], MA[:, c, :], mxh[:, c, :].bitcast(F32), ALU.subtract)\
                    .then_inc(S("mix_ok"), 1)
            dve.wait_ge(S("rwkv_out"), TT)
            def mix_low(h):
                dve.wait_ge(S("mix_hi_ok"), 4 + h + 1)
                dve.tensor_tensor(mxl[:, 4 + h, :], U1[:, h % 2, :], mxh[:, 4 + h, :].bitcast(F32), ALU.subtract)\
                    .then_inc(S("mix_ok"), 1)

            for h in range(HP):
                dve.wait_ge(S("gn_mean"), h + 1)
                dve.scalar_tensor_tensor(U1[:, h % 2, :], bank[4 + h % 2], -1.0 / HD, RX[:, h, :], ALU.mult, ALU.add)\
                    .then_inc(S("gn_centered"), 1)
                if h:
                    mix_low(h - 1)
                dve.wait_ge(S("gn_var_ps"), h + 1)
                dve.tensor_scalar(U2[:, h % 2, :], bank[6 + h % 2], 1.0 / HD, GN_EPS, ALU.mult, ALU.add)\
                    .then_inc(S("gn_var"), 1)
                dve.wait_ge(S("gn_root"), h + 1)
                inverse_root(U3[:, h % 2, :], U2[:, h % 2, :], U4[:, :])
                ch.link(dve.tensor_tensor(U1[:, h % 2, :], U1[:, h % 2, :], U3[:, h % 2, :], ALU.mult))
                ch.link(dve.tensor_scalar(U1[:, h % 2, :], U1[:, h % 2, :], par[:, LNG + h:LNG + h + 1],
                                          par[:, LNB + h:LNB + h + 1], ALU.mult, ALU.add))
                ch.link(dve.tensor_tensor(U1[:, h % 2, :], U1[:, h % 2, :], VX[:, h, :], ALU.add))
                dve.wait_ge(S("gate_out"), h + 1)
                dve.tensor_tensor(U1[:, h % 2, :], U1[:, h % 2, :], G[:, h, :], ALU.mult).then_inc(S("gn_normed"), 1)
            mix_low(HP - 1)
            lo_range(dve, IN_CH + NHL, MOE0)
            dve.wait_ge(S("x_in"), 128)
            dve.wait_ge(w_used, MOE0)
            for tt in range(TT):
                for f in range(2):
                    hs = H[:, tt, 512 * f:512 * f + 512]
                    dve.tensor_tensor(hs, hs, bank[2 * tt + f], ALU.add).then_inc(S("mix_added"), 1)

            dve.wait_ge(S("squares_ok"), 2)
            dve.tensor_scalar(ss[:, 4:8], ss[:, 4:8], 1.0 / D, EPS, ALU.mult, ALU.add).then_inc(S("ms_ok"), 1)
            dve.wait_ge(S("g_ffn_in"), 16)
            dve.wait_ge(S("rms_ok"), 2)
            for tt in range(TT):
                dve.scalar_tensor_tensor(XN2[:, tt, :], H[:, tt, :], rms[:, 4 + tt:5 + tt], g_ffn[:, :],
                                         ALU.mult, ALU.mult).then_inc(S("xn2_ok"), 1)
            dve.wait_ge(S("x2T_ps"), TT)
            for k in range(1, KT, 2):
                dve.tensor_copy(X2T[:, k, :], bank[k]).then_inc(S("x2T_dve"), 1)

            dve.wait_ge(S("logits_ps"), 1)
            ch.link(dve.tensor_tensor(LG[:, :, :], bank[0][:, 0:128].rearrange("p (t e) -> p t e", e=NE),
                                      bc(b_rout[:, :], [P, TT, NE], 1), ALU.add))
            for tt in range(TT):
                ins = dve.max(top8[:, tt, :], LG[:, tt, :])
            ch.link(ins)
            for tt in range(TT):
                dve.max_index(idx8[:, tt, :], top8[:, tt, :], LG[:, tt, :])
            ins = dve.tensor_scalar(ntop[:, :], top8[:, :, 0], -1.0, None, ALU.mult)
            ch.link(ins)
            dve.sem_inc(S("top_ok"), 1)
            ch.link(dve.tensor_copy(idx8f[:, :, :], idx8[:, :, :]))
            ch.link(dve.tensor_tensor(OH[:, :, :, :], idx8f[:, :, 0:4].unsqueeze(3).to_broadcast([P, TT, TOPK, NE]),
                                      iota32[:, :].unsqueeze(1).unsqueeze(1).to_broadcast([P, TT, TOPK, NE]), ALU.is_equal))
            with nc.allow_low_precision("memberships are 0 or 1"):
                dve.reduce_sum(MB[:, :, :], OH[:, :, :, :].rearrange("p t k e -> p t e k"), AXX).then_inc(S("member_ok"), 1)
            dve.wait_ge(S("gate_exp"), 1)
            ch.link(dve.reciprocal(rgs[:, :], gsum[:, :]))
            ch.link(dve.tensor_tensor(gates[:, :, :], gates[:, :, :], bc(rgs[:, :], [P, TT, TOPK], 2), ALU.mult))

            dve.wait_ge(S("rank_ps"), 1)
            cnt = bank[2][:, 0:NE]
            for b in range(4):
                ins = dve.tensor_scalar(nbv[:, b, :], cnt, float(P * b), None, ALU.is_gt)
            ch.link(ins)
            ch.link(dve.reduce_sum(nbl[:, :], nbv[:, :, :].rearrange("p b e -> p e b"), AXX))
            ch.link(dve.tensor_tensor_scan(bend[:, :], onesf[:, :], nbl[:, :], 0.0, ALU.mult, ALU.add))
            ch.link(dve.tensor_tensor(bst[:, :], bend[:, :], nbl[:, :], ALU.subtract))
            ch.link(dve.tensor_scalar(bst[:, :], bst[:, :], float(P), None, ALU.mult))
            ch.link(dve.tensor_tensor(rank[:, :, :], bank[1][:, 0:128].rearrange("p (t e) -> p t e", e=NE),
                                      bc(bst[:, :], [P, TT, NE], 1), ALU.add))
            ch.link(dve.tensor_tensor(dtmp[:, :, :, :], OH[:, :, :, :],
                                      rank[:, :, :].unsqueeze(2).to_broadcast([P, TT, TOPK, NE]), ALU.mult))
            ch.link(dve.reduce_sum(dest[:, :], dtmp[:, :, :, :].rearrange("p t k e -> p (t k) e"), AXX))
            ch.link(dve.tensor_scalar(iotaBx[:, :], iotaB[:, :], float(P), None, ALU.mult))
            NP = TT * TOPK
            ch.link(dve.tensor_tensor(dcmp[:, :, :], bc(dest[:, :], [P, NP, NBT], 2), bc(iotaBx[:, :], [P, NP, NBT], 1),
                                      ALU.is_ge))
            ch.link(dve.reduce_sum(destb[:, :], dcmp[:, :, :], AXX))
            ch.link(dve.tensor_scalar(destb[:, :], destb[:, :], -1.0, None, ALU.add))
            ch.link(dve.scalar_tensor_tensor(destr[:, :], destb[:, :], -float(P), dest[:, :], ALU.mult, ALU.add))
            dve.tensor_tensor(ohR[:, :, :], bc(destr[:, :], [P, NP, P], 2), bc(iotaR[:, :], [P, NP, P], 1), ALU.is_equal)
            ch.link(dve.tensor_tensor(dcmp[:, :, :], bc(destb[:, :], [P, NP, NBT], 2), bc(iotaB[:, :], [P, NP, NBT], 1),
                                      ALU.is_equal))
            for v in range(3):
                ins = dve.tensor_tensor(rhsv[:, v], dcmp[:, :, :], bc(pair_ids[:, v, :], [P, NP, NBT], 2), ALU.mult)
            ins.then_inc(S("pairs_ok"), 1)
            ch.link(dve.tensor_tensor(ecmp[:, :, :], bc(iotaB[:, :], [P, NBT, NE], 2), bc(bend[:, :], [P, NBT, NE], 1),
                                      ALU.is_ge))
            ch.link(dve.reduce_sum(bef[:, :], ecmp[:, :, :], AXX))
            ch.link(dve.tensor_scalar(bef[:, :], bef[:, :], float(NE - 1), None, ALU.min))
            dve.tensor_copy(blk_exp[:, :], bef[:, :])
            dve.tensor_scalar(expsel[:, :], bef[0:96, :], lane32[0:96, :], None, ALU.is_equal)
            dve.tensor_copy(n_blk[:, 0:1], bend[:, NE - 1:NE])
            dve.tensor_scalar(n_blk[:, 1:2], bend[:, NE - 1:NE], -1.0, None, ALU.add)
            dve.wait_ge(S("slots_ps"), 1)
            sp_ = bank[3][:, 0:2 * NBT].rearrange("p (a b) -> p a b", a=2)
            ch.link(dve.tensor_copy(slotv[:, :, :], sp_))
            ch.link(dve.tensor_scalar(skipv[:, :], slotv[:, 1, :], 0.0, SKIP, ALU.is_equal, ALU.mult))
            dve.scalar_tensor_tensor(idx_x[:, :], slotv[:, 0, :], 0.25, skipv[:, :], ALU.mult, ALU.add)
            ch.link(dve.tensor_tensor(slotv[:, 0, :], slotv[:, 0, :], slotv[:, 1, :], ALU.add))
            ch.link(dve.scalar_tensor_tensor(idx_y[:, :], slotv[:, 0, :], -1.0, skipv[:, :], ALU.add, ALU.add))
            dve.sem_inc(S("tables_ok"), 1)

            nb = dve.value_load(n_blk[0:1, 0:1], min_val=16, max_val=NB - 1)
            last_blk = dve.value_load(n_blk[0:1, 1:2], min_val=15, max_val=NB - 2)
            for c in range(8):
                if c == 4:
                    xT_lo(dve, 0, 0)
                xring.make_lo(dve, MOE0 + c, c)
            gate_part(dve, 0)
            block_dve(dve, 0, 0, None)
            block_dve(dve, 1, 1, 0)
            with dve.Fori(0, (NB - 2) // 2) as it:
                for q in range(2):
                    i = it * 2 + (2 + q)
                    with dve.If(i < nb):
                        block_dve(dve, i, q, it * 2 + (1 + q))
            y_dve(dve, nb, last_blk)
            dve.wait_ge(S("y_stored"), nb * 16)
            for tt in range(TT):
                dve.wait_ge(S(f"y_pairs_in{tt % 2}"), 16 * (tt // 2 + 1))
                for k in range(TOPK):
                    ins = dve.scalar_tensor_tensor(H[:, tt, :], YG[:, tt % 2, k, :], gates[:, tt, k:k + 1], H[:, tt, :],
                                                   ALU.mult, ALU.add)
                    if k < TOPK - 1:
                        ch.link(ins)
                ins.then_inc(S("combined"), 1)
                dve.wait_ge(S("squares_final"), tt + 1)
                dve.tensor_scalar(ss[:, 8 + tt:9 + tt], ss[:, 8 + tt:9 + tt], 1.0 / D, EPS, ALU.mult, ALU.add)\
                    .then_inc(S("ms_final"), 1)
                dve.wait_ge(S("rms_final"), tt + 1)
                dve.wait_ge(S("g_fin_in"), 16)
                if tt >= 2:
                    dve.wait_ge(S("final_free"), tt - 1)
                dve.scalar_tensor_tensor(FO[:, tt % 2, :], H[:, tt, :], rms[:, 8 + tt:9 + tt], g_fin[:, :],
                                         ALU.mult, ALU.mult).then_inc(S("final_ok"), 1)


        def att_flip(pe, qt, pe_probs):
            pe.wait_ge(S("att_on"), qt + 1)
            pe.wait_ge(S("probsT_ok"), pe_probs)
            on = ON[:, :, :].rearrange("p h d -> p (h d)")
            for c in range(4):
                last = pe.matmul(bank[4][:, c * P:(c + 1) * P], on[:, c * P:(c + 1) * P], ident[:, :],
                                 start=True, stop=True, is_transpose=True)
            last.then_inc(S("attT_ps"), 1)

        @block.tensor
        def _(pe):
            def flip(o, i, n=P):
                return pe.matmul(o, i, ident[0:n, 0:n], start=True, stop=True, is_transpose=True)

            pe.wait_ge(S("ident_ok"), 1)
            pe.wait_ge(S("params_in"), 16 * NPAR)
            pe.wait_ge(S("squares_ok"), 1)
            flip(bank[7][:, 0:48], par_rows[:, :], 48).then_inc(S("param_ps"), 1)
            pe.wait_ge(S("params_ok"), 1)
            for tt in range(TT):
                pe.wait_ge(S("xs_ok"), tt + 1)
                for k in range(KT):
                    last = flip(bank[k][:, tt * P:(tt + 1) * P], xs[:, tt % 2, k::KT])
                last.then_inc(S("xT_first"), 1)

            pe.wait_ge(S("xnl_ok"), KT)
            for g in range(6):
                b0 = (g % 2) * 4
                if g in (2, 4):
                    pe.wait_ge(S("qv_out"), g // 2)
                if g == 3:
                    pe.wait_ge(S("group1_out"), 1)
                if g == 5:
                    pe.wait_ge(S("unshifted_ok"), 4)
                for q in range(4):
                    n = 4 * g + q
                    pe.wait_ge(lo_done, n + 1)
                    wh = whi[:, n % NHL, :].rearrange("p (k n) -> p k n", k=2)
                    wl = wlo[:, n % NHL, :].rearrange("p (k n) -> p k n", k=2)
                    for c in range(4):
                        for j in range(2):
                            k = 2 * q + j
                            start, stop = k == 0, k == KT - 1
                            cs = slice(c * P, (c + 1) * P)
                            if g == 2:
                                last = three(pe, bank[b0 + c], wh[:, j, :], wl[:, j, :], xnh[:, k, cs], xnl[:, k, cs],
                                             start, stop, True)
                            else:
                                last = three(pe, bank[b0 + c], wh[:, j, cs], wl[:, j, cs], xnh[:, k, :], xnl[:, k, :],
                                             start, stop, False)
                    last.then_inc(w_used, 1)
            pe.wait_ge(S("unshifted_ok"), 8)
            for q in range(2):
                n = 24 + q
                pe.wait_ge(lo_done, n + 1)
                wh = whi[:, n % NHL, 0:640].rearrange("p (k n) -> p k n", k=4)
                wl = wlo[:, n % NHL, 0:640].rearrange("p (k n) -> p k n", k=4)
                for o, cs in ((bank[0], slice(0, P)), (bank[1][0:96, :], slice(64, 160))):
                    for j in range(4):
                        k = 4 * q + j
                        last = three(pe, o, wh[:, j, cs], wl[:, j, cs], xnh[:, k, :], xnl[:, k, :], k == 0, k == KT - 1,
                                     False)
                last.then_inc(w_used, 1)

            pe.wait_ge(S("unshifted_ok"), 14)
            pe.wait_ge(S("group1_out"), 1)
            pe.wait_ge(S("qv_out"), 2)
            for u in range(16 + 3):
                if u < 16:
                    qt, h = u // 4, u % 4
                    nk = (qt + 1) * P
                    if u >= 2:
                        pe.wait_ge(S("scores_ok"), u - 1)
                    for j in range(2):
                        r = slice(64 * j, 64 * j + 64)
                        last = pe.matmul(bank[2 * (u % 2) + j][:, 0:nk], QT[r, h, qt * P:(qt + 1) * P], KTT[r, h, 0:nk],
                                         start=True, stop=True)
                    last.then_inc(S("scores_ps"), 1)
                if u >= 3:
                    v = u - 3
                    qt = v // 4
                    pe.wait_ge(S("probsT_ok"), v + 1)
                    if v % 4 == 0 and qt >= 2:
                        pe.wait_ge(S("att_on"), qt - 1)
                    for j in range(2):
                        h = 2 * (v % 4) + j
                        for c in range(qt + 1):
                            last = pe.matmul(bank[6 + qt % 2][:, h * HD:(h + 1) * HD], PRT[:, v % 2, j, c * P:(c + 1) * P],
                                             VA[:, c, h * HD:(h + 1) * HD], start=c == 0, stop=c == qt)
                    last.then_inc(S("att_pv"), 1)
                if 2 <= u < 18:
                    v = u - 2
                    pe.wait_ge(S("probs_ok"), v + 1)
                    if v >= 1:
                        pe.wait_ge(S("probsT_ok"), v)
                    if v % 4 == 3 and v > 4:
                        att_flip(pe, v // 4 - 1, v)
                        pe.wait_ge(S("att_gained"), v // 4)
                    for j in range(2):
                        for c in range(v // 4 + 1):
                            last = flip(bank[4 + j][:, c * P:(c + 1) * P], PR[:, v % 2, j, c * P:(c + 1) * P])
                    last.then_inc(S("probsT_ps"), 1)
            att_flip(pe, 3, 16)

            pe.wait_ge(S("lora_in"), 1)
            pe.wait_ge(S("att_done"), 1)
            for h in range(HP):
                cs = slice(h * P, (h + 1) * P)
                pe.matmul(bank[h], w2a2[0:32, cs], TL[:, :], start=True, stop=True)
                pe.matmul(bank[4 + h], w2a2[32:64, cs], XL[32:64, 0, :], start=True, stop=True).then_inc(S("lora_ps"), 1)
            for h in range(HP):
                pe.wait_ge(S("kk_sq"), h + 1)
                pe.wait_ge(S("sig_ok"), h + 1)
                pe.matmul(bank[h], head_ones[:, :], T4[:, h % 2, :], start=True, stop=True).then_inc(S("kk_ss_ps"), 1)
            pe.wait_ge(S("prep_done"), 1)
            pe.wait_ge(S("state_written"), 1)

            with pe.Fori(0, TT) as tt:
                pe.wait_ge(S("ab_tile"), tt + 1)
                pe.wait_ge(S("kr_tile"), tt + 1)
                pe.wait_ge(S("v_tile"), tt + 1)
                for b, t in enumerate((ASt, BSt, KSt, VSt)):
                    for h in range(HP):
                        last = flip(bank[b][:, h * P:(h + 1) * P], t[:, h, :])
                last.then_inc(S("rows_ps"), 1)

                def products(banks, left, right):
                    for h in range(HP):
                        for j in range(2):
                            r = slice(64 * j, 64 * j + 64)
                            last = pe.matmul(bank[banks + j][:, h * P:(h + 1) * P], left[r, h, :], right[r, h, :],
                                             start=True, stop=True)
                    return last

                products(4, BSt, ASt)
                products(6, ASt, BSt).then_inc(S("AT_ps"), 1)
                pe.wait_ge(S("a_rows"), tt + 1)
                pe.wait_ge(S("bkv_rows"), tt + 1)
                products(0, KSt, ASt)
                products(2, BSt, RSt).then_inc(S("TK_ps"), 1)
                pe.wait_ge(S("AT_ok"), tt + 1)
                pe.wait_ge(S("inv_ok"), tt * 12 + 2)
                products(4, KSt, RSt).then_inc(S("RK_ps"), 1)
                pe.wait_ge(S("bonus_prod"), tt + 1)
                pe.matmul(bank[6], head_ones[:, :], BP[:, :, :].rearrange("p h t -> p (h t)"), start=True, stop=True)\
                    .then_inc(S("bonus_ps"), 1)
                pe.wait_ge(S("TK_ok"), tt + 1)
                pe.wait_ge(S("RB_ok"), tt + 1)
                pe.wait_ge(S("RK_ok"), tt + 1)

                for l in range(1, 6):
                    for j in range(2):
                        pe.wait_ge(S("inv_ok"), tt * 12 + (2 * l + j - 1) if l > 1 else tt * 12 + 2)
                        for h in range(HP):
                            last = pe.matmul(bank[j][:, h * P:(h + 1) * P], AsT[:, j, h, :], Xi[:, j, h, :],
                                             start=True, stop=True)
                        last.then_inc(S("step_ps"), 1)
                    if l == 1:
                        pe.wait_ge(S("bonus_ok"), tt + 1)
                        for h in range(8):
                            last = pe.matmul(bank[6][:, h * CH:(h + 1) * CH], TKm[:, h % 2, h // 2, :],
                                             Vt[:, h * CH:(h + 1) * CH], start=True, stop=True)
                        last.then_inc(S("z0_ps"), 1)
                    for j in range(2):
                        pe.wait_ge(S("step_ok"), tt * 10 + (2 * (l - 1) + j + 1))
                        for h in range(HP):
                            if l < 5:
                                pe.matmul(bank[2 + j][:, h * P:(h + 1) * P], XiT[:, j, h, :], Pm[:, j, h, :],
                                          start=True, stop=True)
                            last = pe.matmul(bank[4 + j][:, h * P:(h + 1) * P], Pm[:, j, h, :], XiT[:, j, h, :],
                                             start=True, stop=True)
                        last.then_inc(S("inv_ps"), 1)
                pe.wait_ge(S("z0_rows"), tt + 1)
                pe.wait_ge(S("inv_ok"), tt * 12 + 12)
                for h in range(8):
                    last = pe.matmul(bank[6 + h % 2][:, (h // 2) * P:(h // 2 + 1) * P], XiT[:, h % 2, h // 2, :],
                                     AZ[:, h, :, :].rearrange("p c d -> p (c d)"), start=True, stop=True)
                last.then_inc(S("uz_ps"), 1)
                pe.wait_ge(S("uz_rows"), tt + 1)
                for c in range(2):
                    r = slice(64 * c, 64 * c + 64)
                    for h in range(HP):
                        last = pe.matmul(bank[1 + c][:, h * P:(h + 1) * P], UZ[r, 0, 2 * h:2 * h + 2, :].rearrange("p h d -> p (h d)"),
                                         Bt[r, h * P:(h + 1) * P], start=True, stop=True)
                last.then_inc(S("map_ps"), 1)
                for h in range(8):
                    j = h % 2
                    last = pe.matmul(bank[0][64 * j:64 * j + 64, (h // 2) * P:(h // 2 + 1) * P], UZ[:, 0, h, :],
                                     RBm[:, j, h // 2, :], start=True, stop=True)
                last.then_inc(S("r2_ps"), 1)
                for c in range(2):
                    r = slice(64 * c, 64 * c + 64)
                    for h in range(HP):
                        o = bank[3 + c][:, h * P:(h + 1) * P]
                        pe.matmul(o, Bt[r, h * P:(h + 1) * P], UZ[r, 1, 2 * h:2 * h + 2, :].rearrange("p h d -> p (h d)"), start=True, stop=False)
                        last = pe.matmul(o, Kt[r, h * P:(h + 1) * P], Vt[r, h * P:(h + 1) * P], start=False, stop=True)
                last.then_inc(S("add_ps"), 1)
                for h in range(8):
                    j = h % 2
                    o = bank[5][64 * j:64 * j + 64, (h // 2) * P:(h // 2 + 1) * P]
                    pe.matmul(o, UZ[:, 1, h, :], RBm[:, j, h // 2, :], start=h < 2, stop=False, skip_group_check=True)
                    pe.matmul(o, Vt[:, h * CH:(h + 1) * CH], RKm[:, j, h // 2, :], start=False, stop=False,
                              skip_group_check=True)
                pe.wait_ge(S("r2_ok"), tt + 1)
                for c in range(2):
                    if c == 1:
                        pe.wait_ge(S("state_written"), tt * 2 + 2)
                    for h in range(HP):
                        last = pe.matmul(bank[5][:, h * P + 64 * c:h * P + 64 * c + 64], ST[:, h, :],
                                         R2[:, h, 64 * c:64 * c + 64], start=False, stop=c == 1, skip_group_check=True)
                    if c == 1:
                        last.then_inc(S("out_ps"), 1)
                    else:
                        pe.wait_ge(S("map_ok"), tt + 1)
                    for h in range(HP):
                        last = pe.matmul(bank[6 + c][:, h * P:(h + 1) * P], MTm[:, c, h, :], ST[:, h, :],
                                         start=True, stop=True)
                    last.then_inc(S("chain_ps"), 1)

            pe.wait_ge(S("state_written"), 2 * TT + 1)
            pe.wait_ge(S("rwkv_out"), TT)
            for h in range(HP):
                pe.matmul(bank[h], g2[:, h * P:(h + 1) * P], XL[0:96, 1, :], start=True, stop=True)\
                    .then_inc(S("gate_ps"), 1)
            for h in range(HP):
                if h >= 2:
                    pe.wait_ge(S("gn_centered"), h - 1)
                pe.matmul(bank[4 + h % 2], head_ones[:, :], RX[:, h, :], start=True, stop=True).then_inc(S("gn_mean"), 1)
                pe.wait_ge(S("gn_sq"), h + 1)
                if h >= 2:
                    pe.wait_ge(S("gn_var"), h - 1)
                pe.matmul(bank[6 + h % 2], head_ones[:, :], U2[:, h % 2, :], start=True, stop=True)\
                    .then_inc(S("gn_var_ps"), 1)
            pe.wait_ge(S("gn_var"), HP)
            pe.wait_ge(S("gn_centered"), HP)
            pe.wait_ge(S("gate_out"), HP)
            for c in range(OUT_CH):
                n = IN_CH + c
                pe.wait_ge(lo_done, n + 1)
                pe.wait_ge(S("mix_ok"), c + 1)
                for tt in range(TT):
                    for f in range(2):
                        ts, fs = slice(tt * P, (tt + 1) * P), slice(512 * f, 512 * f + 512)
                        last = three(pe, bank[2 * tt + f], whi[:, n % NHL, fs], wlo[:, n % NHL, fs], mxh[:, c, ts],
                                     mxl[:, c, ts], c == 0, c == OUT_CH - 1, True)
                last.then_inc(w_used, 1)

            pe.wait_ge(S("mix_added"), 8)
            for tt in range(TT):
                pe.wait_ge(S("xn2_ok"), tt + 1)
                for k in range(KT):
                    last = flip(bank[k][:, tt * P:(tt + 1) * P], XN2[:, tt, k::KT])
                last.then_inc(S("x2T_ps"), 1)
            pe.wait_ge(S("x2T_act"), KT // 2)
            pe.wait_ge(S("x2T_dve"), KT // 2)
            for tt in range(TT):
                for k in range(KT):
                    last = pe.matmul(bank[0][:, tt * NE:(tt + 1) * NE], X2T[:, k, tt * P:(tt + 1) * P], w_rout[:, k, :],
                                     start=k == 0, stop=k == KT - 1)
            last.then_inc(S("logits_ps"), 1)
            pe.wait_ge(S("member_ok"), 1)
            for tt in range(TT):
                for t2 in range(tt + 1):
                    pe.matmul(bank[1][:, tt * NE:(tt + 1) * NE], (triu if t2 == tt else ones_b)[:, :], MB[:, t2, :],
                              start=t2 == 0, stop=t2 == tt)
            for tt in range(TT):
                last = pe.matmul(bank[2][:, 0:NE], ones_b[:, :], MB[:, tt, :], start=tt == 0, stop=tt == TT - 1)
            last.then_inc(S("rank_ps"), 1)
            pe.wait_ge(S("pairs_ok"), 1)
            NP = TT * TOPK
            for half, parts in ((0, (0, 1)), (1, (2,))):
                seq = [(v, m) for v in parts for m in range(NP)]
                for z, (v, m) in enumerate(seq):
                    last = pe.matmul(bank[3][:, half * NBT:(half + 1) * NBT], ohR[:, m, :], rhsv[:, v, m, :],
                                     start=z == 0, stop=z == len(seq) - 1)
            last.then_inc(S("slots_ps"), 1)

            pe.wait_ge(S("tables_ok"), 1)
            nb = pe.value_load(n_blk[0:1, 0:1], min_val=16, max_val=NB - 1)

            def bias(o, w, f, last_of=False):
                return pe.matmul(o, bsel[:, :], biasb[:, w, 512 * f:512 * f + 512], start=True, stop=False)

            def chunk(n, k, o, xh, xl, kt):
                pe.wait_ge(lo_done, n + 1)
                for f in range(2):
                    fs = slice(512 * f, 512 * f + 512)
                    last = three(pe, o[:, fs], whi2[:, k % NHL2, fs], wlo2[:, k % NHL2, fs], xh[:, kt, :], xl[:, kt, :],
                                 False, kt == KT - 1, True)
                last.then_inc(w_used, 1)

            def block_transpose(src, done):
                for k in range(KT):
                    last = flip(bank[6 + k // 4][:, (k % 4) * P:(k % 4 + 1) * P], src[:, k::KT])
                last.then_inc(done, 1)

            pe.wait_ge(S("xb_in0"), 16)
            block_transpose(XB[:, 0, :], S("xT_ps"))
            pe.wait_ge(S("bias_sel"), 1)
            for f in range(2):
                last = bias(bank[f], 0, f)
            for c in range(8):
                if c == 0:
                    pe.wait_ge(S("xT_ok"), 1)
                chunk(MOE0 + c, c, pair[0], xbh[0], xbl[0], c)

            def xb_turn(j, q):
                return (j // 2 + 1) if isinstance(j, int) else (j + (1 if q else 2)) // 2

            def block_pe(i, q, prev):
                base, k0 = MOE0 + 8 + i * PER, 8
                if prev is not None:
                    pe.wait_ge(S("up_ok"), i)
                for f in range(2):
                    bias(bank[2 + f], 1, f)
                for c in range(8):
                    chunk(base + c, k0 + c, pair[1], xbh[q], xbl[q], c)
                    if c == 2:
                        if prev is not None:
                            pe.wait_ge(S("y_act"), i)
                            pe.wait_ge(S("y_dve"), i)
                        for f in range(2):
                            last = bias(bank[4 + f], 2, f)
                        last.then_inc(S("up_down_bias"), 1)
                    if c == 3:
                        pe.wait_ge(S(f"xb_in{1 - q}"), xb_turn(i + 1, 1 - q) * 16)
                        if prev is not None:
                            pe.wait_ge(S("hT_ok"), i)
                        block_transpose(XB[:, 1 - q, :], S("xT_ps"))
                pe.wait_ge(S("gate_ok"), i + 1)
                pe.wait_ge(S("bias_sel"), i + 2)
                for f in range(2):
                    bias(bank[f], 0, f)
                pe.wait_ge(S("xT_ok"), i + 2)
                for c in range(8):
                    chunk(base + (8 + c), k0 + 8 + c, pair[0], xbh[1 - q], xbl[1 - q], c)
                    if c == 4:
                        pe.wait_ge(S("h_ok"), i + 1)
                        block_transpose(HB[:, :], S("hT_ps"))
                pe.wait_ge(S("hT_ok"), i + 1)
                for c in range(8):
                    chunk(base + (16 + c), k0 + 16 + c, pair[2], hbh, hbl, c)

            block_pe(0, 0, None)
            block_pe(1, 1, 0)
            with pe.Fori(0, (NB - 2) // 2) as it:
                for q in range(2):
                    i = it * 2 + (2 + q)
                    with pe.If(i < nb):
                        block_pe(i, q, it * 2 + (1 + q))



_INS = ["x", "norm_mix_g", "w_in", "attn_norm_g", "rwkv_mu", "rwkv_w0", "rwkv_w2", "rwkv_a0", "rwkv_a2", "rwkv_g2",
        "rwkv_k_k", "rwkv_k_a", "rwkv_r_k", "rwkv_ln_g", "rwkv_ln_b", "w_out", "norm_ffn_g", "w_router", "b_router",
        "moe_w_gate", "moe_b_gate", "moe_w_up", "moe_b_up", "moe_w_down", "moe_b_down", "norm_final_g"]


def kernel(**inputs):
    import numpy as _np
    import concourse.bacc as _bacc
    from concourse import mybir as _mybir
    from concourse.bass_utils import run_bass_kernel_spmd as _run

    nc = _bacc.Bacc("TRN2", target_bir_lowering=False, num_devices=1)
    arrays, aps = {}, {}
    for name in _INS:
        a = _np.ascontiguousarray(inputs[name])
        arrays[f"in_{name}_dram"] = a
        aps[name] = nc.dram_tensor(f"in_{name}_dram", a.shape, _mybir.dt.from_np(a.dtype), kind="ExternalInput").ap()
    out = nc.dram_tensor("out_0_dram", (1, 512, 1024), _mybir.dt.float32, kind="ExternalOutput").ap()
    hymba_block(nc, aps, out)
    r = _run(nc, [arrays], core_ids=[0])
    return r.results[0]["out_0_dram"]
```

```python
import math
from contextlib import ExitStack

import concourse.bass as bass
from concourse import mybir


def hymba_block(nc, t_in, out):
    F32, F32R, BF16 = mybir.dt.float32, mybir.dt.float32r, mybir.dt.bfloat16
    I32, U32 = mybir.dt.int32, mybir.dt.uint32
    ALU = mybir.AluOpType
    ACT = mybir.ActivationFunctionType
    AXX = mybir.AxisListType.X
    ds = bass.ds

    P = 128
    D, SEQ, HD = 1024, 512, 64
    TT = SEQ // P
    KT = D // P
    HP = 4
    CH = 64
    NE, TOPK = 32, 4
    NB = SEQ * TOPK // P + NE
    C = 1024
    NRAW, NHL = 6, 4
    NRAW2, NHL2 = 12, 8
    IN_CH, OUT_CH = 26, 8
    MOE0 = IN_CH + OUT_CH
    PER = 24
    DECAY = math.exp(-0.5)
    EPS, GN_EPS = 1e-6, HD * 1e-5
    LIMIT, ALPHA = 7.0, 1.702
    SKIP = 1.0e6
    NBT = NB + 2

    MU, W0, A0, KK_, KA_, RK_, LNG, LNB, ATG = 0, 14, 18, 22, 26, 30, 34, 38, 42
    NPAR = 17

    x_d = t_in["x"][0]
    w_in_v = t_in["w_in"][0].rearrange("(p k) n -> p k n", k=KT)
    w_out_v = t_in["w_out"][0].rearrange("(c p) n -> p c n", p=P)
    wg_v = t_in["moe_w_gate"].rearrange("l e (p k) f -> (l e) p (k f)", k=KT)
    wu_v = t_in["moe_w_up"].rearrange("l e (p k) f -> (l e) p (k f)", k=KT)
    wd_v = t_in["moe_w_down"].rearrange("l e (p k) f -> (l e) p (k f)", k=KT)

    ctx = ExitStack()

    def sb(name, shape, dt=F32, scope=None):
        return (scope or ctx).enter_context(nc.sbuf_tensor(name, shape, dt))

    with ctx:
        pair = [ctx.enter_context(nc.psum_tensor(f"banks{2 * i}_{2 * i + 1}", [P, 1024], F32)) for i in range(4)]
        bank = [pair[i // 2][:, (i % 2) * 512:(i % 2) * 512 + 512] for i in range(8)]

        H = sb("residual", [P, TT, D])
        biasb = sb("expert_bias_parts", [96, 3, D], BF16)
        ident = sb("ident", [P, P])
        ss = sb("sum_squares", [P, 3 * TT])
        rms = sb("rms_scale", [P, 3 * TT])
        neghalf = sb("neg_half", [P, 1])
        iota32 = sb("iota_experts", [P, NE])
        onesf = sb("ones_experts", [P, NE])
        b_rout = sb("b_router_rows", [P, NE])
        w_rout = sb("w_router", [P, KT, NE])
        triu = sb("tri_strict", [P, P], BF16)
        ones_b = sb("ones_b", [P, P], BF16)
        iotaB = sb("iota_blocks", [P, NBT])
        iotaR = sb("iota_rows", [P, P])
        pair_ids = sb("pair_ids", [P, 3, TT * TOPK])
        lane32 = sb("lane_mod_32", [P, 1])
        blk_exp = sb("block_expert", [P, NBT], I32)
        n_blk = sb("n_blocks", [P, 2], I32)
        expsel = sb("expert_selector", [96, NBT], BF16)
        idx_x = sb("slot_token", [P, NBT], I32)
        idx_y = sb("slot_pair", [P, NBT], I32)
        gates = sb("gates", [P, TT, TOPK])

        pre = ExitStack()
        raw = sb("w_raw", [P, NRAW, C], scope=pre)
        whi = sb("w_hi", [P, NHL, C], F32R, scope=pre)
        wlo = sb("w_lo", [P, NHL, C], F32R, scope=pre)
        par_rows = sb("param_rows", [48, P], scope=pre)
        par = sb("params", [P, 48], scope=pre)
        one_m_ka = sb("one_minus_k_a", [P, HP], scope=pre)
        g_mix = sb("norm_mix_g", [P, KT], scope=pre)
        w2a2 = sb("w2_a2", [64, 512], scope=pre)
        g2 = sb("g2", [96, 512], scope=pre)
        head_ones = sb("head_ones", [P, P], scope=pre)
        mask_su = sb("mask_s_lt_t", [P, P], scope=pre)
        mask_iu = sb("mask_s_le_t", [P, P], scope=pre)
        sel_T = sb("head_selector_T", [8, 512], scope=pre)
        n_k_k = sb("minus_k_k", [P, HP], scope=pre)
        NV = sb("norm_in", [P, 8 * TT], scope=pre)
        NR = sb("norm_inverse", [P, 8 * TT], scope=pre)
        NT = sb("norm_newton", [P, 8 * TT], scope=pre)
        lvl = sb("level_masks", [P, 6, P], scope=pre)
        lvl0T = sb("level0_mask_T", [P, P], scope=pre)
        dist = sb("minus_distance", [P, 512], scope=pre)
        SCM = sb("scan_mult", [P, 8 * 65], scope=pre)
        RX = sb("r_shifted", [P, HP, 512], scope=pre)
        KX = sb("k_shifted", [P, HP, 512], scope=pre)
        VX = sb("v_shifted", [P, HP, 512], scope=pre)
        XL = sb("lora_shifted", [P, 2, 512], scope=pre)
        xs = sb("x_scaled", [P, 2, D], scope=pre)
        MA = xs[:, :, :].rearrange("p a (b t) -> p (a b) t", b=2)

        q_scope = ExitStack()
        QT = sb("qT", [P, HP, 512], scope=q_scope)
        KTT = sb("kT", [P, HP, 512], scope=q_scope)
        VA = sb("v_att", [P, TT, 512], scope=q_scope)
        a_scope = ExitStack()
        xnh = sb("xn_hi", [P, KT, 512], F32R, scope=a_scope)
        xnl = sb("xn_lo", [P, KT, 512], F32R, scope=a_scope)
        XR = sb("x_unshifted", [P, 2, 513], scope=a_scope)
        DF = sb("x_shift_diff", [P, 2, 512], scope=a_scope)
        bias_raw = sb("expert_bias_words", [96, D], scope=a_scope)
        a_scope.close()
        SC = sb("scores", [P, 2, 2, 512], scope=q_scope)
        PR = sb("probs", [P, 2, 2, 512], scope=q_scope)
        PRT = sb("probs_T", [P, 2, 2, 512], scope=q_scope)
        nmax = sb("neg_row_max", [P, 32], scope=q_scope)
        rsum = sb("row_sum", [P, 32], scope=q_scope)
        rinv = sb("row_rinv", [P, 32], scope=q_scope)
        ON = sb("att_norm", [P, 8, HD], scope=q_scope)
        OSQ = sb("att_sq", [P, 8, HD], scope=q_scope)
        hss = sb("att_head_ss", [P, TT, 8], scope=q_scope)
        hrs = sb("att_head_rms", [P, TT, 8], scope=q_scope)
        q_scope.close()

        r_scope = ExitStack()
        KKN = sb("minus_kk", [P, HP, 512], scope=r_scope)
        BV = sb("b_vec", [P, HP, 512], scope=r_scope)
        CS = sb("decay_cumsum", [P, HP, 8, CH + 1], scope=r_scope)
        p_scope = ExitStack()
        T4 = sb("kk_sq", [P, HP, 512], scope=p_scope)
        SIG = sb("decay_sigmoid", [P, HP, 8, CH + 1], scope=p_scope)
        TL = sb("tanh_lora", [32, 512], scope=p_scope)
        AV = sb("a_vec", [P, HP, 512], scope=p_scope)
        T1 = sb("k_factor", [P, 2, 512], scope=p_scope)
        NRT0 = sb("kk_inverse_T", [8, 512], scope=p_scope)
        p_scope.close()
        l_scope = ExitStack()
        DEC = sb("chunk_decay", [P, HP, 2, 1], scope=l_scope)
        E01 = sb("exp_cs", [P, HP, 2, CH + 1], scope=l_scope)
        EI = sb("exp_neg_cs", [P, HP, 2, CH], scope=l_scope)
        ASt = sb("a_tile", [P, HP, P], scope=l_scope)
        BSt = sb("b_tile", [P, HP, P], scope=l_scope)
        KSt = sb("k_tile", [P, HP, P], scope=l_scope)
        RSt = sb("r_tile", [P, HP, P], scope=l_scope)
        VSt = sb("v_tile", [P, HP, P], scope=l_scope)
        BP = sb("bonus_product", [P, HP, P], scope=l_scope)
        Bt = sb("b_rows", [P, 512], scope=l_scope)
        Kt = sb("k_rows", [P, 512], scope=l_scope)
        Vt = sb("v_rows", [P, 512], scope=l_scope)
        AZ = sb("a_z0_rows", [P, 8, 2, CH], scope=l_scope)
        TKm = sb("TK_T", [P, 2, HP, P], scope=l_scope)
        RBm = sb("RB_T", [P, 2, HP, P], scope=l_scope)
        RKm = sb("RK_T", [P, 2, HP, P], scope=l_scope)
        UZ = sb("u_z_rows", [P, 2, 8, CH], scope=l_scope)
        R2 = sb("r2_T", [P, HP, P], scope=l_scope)
        SN = sb("state_sum", [P, HP, P], scope=l_scope)
        ST = sb("state_T", [P, HP, P], scope=l_scope)
        l_scope.close()
        AsT, Xi, XiT, Pm = (H[:, k, :].rearrange("p (j h t) -> p j h t", j=2, h=HP) for k in range(4))
        MTm, NN = Pm, AsT
        r_scope.close()
        o_scope = ExitStack()
        G = sb("gate_T", [P, HP, 512], scope=o_scope)
        GG = sb("gate_gain_T", [P, HP, 512], scope=o_scope)
        U2 = sb("gn_sq", [P, HP, 512], scope=o_scope)
        NRT1 = sb("gn_inverse_T", [8, 512], scope=o_scope)
        mxh = sb("mix_hi", [P, 8, 512], F32R, scope=o_scope)
        mxl = sb("mix_lo", [P, 8, 512], F32R, scope=o_scope)
        o_scope.close()
        pre.close()

        g_ffn = sb("norm_ffn_g", [P, D])
        raw2 = sb("expert_w_raw", [P, NRAW2, C])
        whi2 = sb("expert_w_hi", [P, NHL2, C], F32R)
        wlo2 = sb("expert_w_lo", [P, NHL2, C], F32R)
        rt = ExitStack()
        XN2 = sb("xn2", [P, TT, D], scope=rt)
        X2T = sb("xn2_T", [P, KT, 512], scope=rt)
        LG = sb("logits", [P, TT, NE], scope=rt)
        top8 = sb("top8", [P, TT, 8], scope=rt)
        idx8 = sb("idx8", [P, TT, 8], U32, scope=rt)
        idx8f = sb("idx8f", [P, TT, 8], scope=rt)
        OH = sb("onehot", [P, TT, TOPK, NE], scope=rt)
        MB = sb("member", [P, TT, NE], BF16, scope=rt)
        gsum = sb("gate_sum", [P, TT], scope=rt)
        ntop = sb("neg_top", [P, TT], scope=rt)
        rgs = sb("gate_rsum", [P, TT], scope=rt)
        nbv = sb("blocks_parts", [P, 4, NE], scope=rt)
        nbl = sb("blocks_of_expert", [P, NE], scope=rt)
        bend = sb("block_end", [P, NE], scope=rt)
        bst = sb("slot_start", [P, NE], scope=rt)
        rank = sb("slot_of_expert", [P, TT, NE], scope=rt)
        dtmp = sb("dest_parts", [P, TT, TOPK, NE], scope=rt)
        dest = sb("dest", [P, TT * TOPK], scope=rt)
        destb = sb("dest_block", [P, TT * TOPK], scope=rt)
        destr = sb("dest_row", [P, TT * TOPK], scope=rt)
        dcmp = sb("dest_cmp", [P, TT * TOPK, NBT], scope=rt)
        ohR = sb("onehot_row", [P, TT * TOPK, P], BF16, scope=rt)
        rhsv = sb("pair_value", [P, 3, TT * TOPK, NBT], BF16, scope=rt)
        ecmp = sb("expert_cmp", [P, NBT, NE], scope=rt)
        bef = sb("block_expert_f", [P, NBT], scope=rt)
        slotv = sb("slot_value", [P, 2, NBT], scope=rt)
        skipv = sb("slot_skip", [P, NBT], scope=rt)
        rt.close()

        mo = ctx.enter_context(ExitStack())
        XB = sb("x_block", [P, 2, D], scope=mo)
        xbh = [sb(f"x_block_T_hi{q}", [P, KT, P], F32R, scope=mo) for q in range(2)]
        xbl = [sb(f"x_block_T_lo{q}", [P, KT, P], F32R, scope=mo) for q in range(2)]
        now_x = [sb(f"gather_rows{q}", [P, 1], I32, scope=mo) for q in range(2)]
        now_y = sb("scatter_rows", [P, 1], I32, scope=mo)
        bsel = sb("bias_selector", [96, P], BF16, scope=mo)
        GT = sb("gate_act", [P, D], scope=mo)
        SG = sb("gate_sigmoid", [P, D], scope=mo)
        UP = sb("up_act", [P, D], scope=mo)
        HB = sb("h_block", [P, D], scope=mo)
        hbh = sb("h_block_T_hi", [P, KT, P], F32R, scope=mo)
        hbl = sb("h_block_T_lo", [P, KT, P], F32R, scope=mo)
        YB = sb("y_block", [P, D], scope=mo)
        YG = raw2[:, 0:2 * TOPK, :].rearrange("p (a k) d -> p a k d", a=2)
        g_fin = sb("norm_final_g", [P, D], scope=mo)
        FO = XB

        xn2_d = nc.dram_tensor("xn2_rows", (SEQ, D), F32, kind="Internal").ap()
        y_d = nc.dram_tensor("y_pair_rows", (SEQ * TOPK, D), F32, kind="Internal").ap()

        sems = {}

        def S(name):
            if name not in sems:
                sems[name] = ctx.enter_context(nc.semaphore(name))
            return sems[name]

        class Chain:

            def __init__(self, eng, name):
                self.eng, self.sem, self.base, self.n = eng, S(name), 0, 0

            def link(self, ins):
                self.n += 1
                ins.then_inc(self.sem, 1)
                self.eng.wait_ge(self.sem, self.base + self.n)

        hi_done, lo_done, w_used = S("hi_done"), S("lo_done"), S("weights_used")

        class Ring:

            def __init__(self, raw_, hi_, lo_, nraw, nhl, start, before):
                self.raw, self.hi, self.lo, self.nraw, self.nhl = raw_, hi_, lo_, nraw, nhl
                self.landed = [S(f"weights_in_{i}") for i in range(nraw)]
                self.start = start
                self.before = before

            def load(self, sp, n, k, src, view=None):
                if not isinstance(n, int) or n >= self.start + self.nraw:
                    sp.wait_ge(lo_done, n - (self.nraw - 1))
                dst = self.raw[:, k % self.nraw, :]
                sp.dma_start(dst if view is None else view(dst), src).then_inc(self.landed[k % self.nraw], 16)

            def make_hi(self, act, n, k, turn, width=C):
                act.wait_ge(self.landed[k % self.nraw], 16 * (turn + 1 + self.before[k % self.nraw]))
                if not isinstance(n, int) or n >= self.start + self.nhl:
                    act.wait_ge(w_used, n - (self.nhl - 1))
                act.activation(self.hi[:, k % self.nhl, 0:width], self.raw[:, k % self.nraw, 0:width], ACT.Copy)\
                    .then_inc(hi_done, 1)

            def make_lo(self, dve, n, k, width=C):
                dve.wait_ge(hi_done, n + 1)
                dve.tensor_tensor(self.lo[:, k % self.nhl, 0:width], self.raw[:, k % self.nraw, 0:width],
                                  self.hi[:, k % self.nhl, 0:width].bitcast(F32), ALU.subtract).then_inc(lo_done, 1)

        ring = Ring(raw, whi, wlo, NRAW, NHL, 0, [0] * NRAW)
        xring = Ring(raw2, whi2, wlo2, NRAW2, NHL2, MOE0,
                     [len(range(i, MOE0, NRAW)) if i < NRAW else 0 for i in range(NRAW2)])

        def in_width(n):
            return C if n < 24 else 4 * 160

        def hi_range(act, a, b):
            for n in range(a, b):
                ring.make_hi(act, n, n, n // NRAW, in_width(n) if n < IN_CH else C)

        def lo_range(dve, a, b):
            for n in range(a, b):
                ring.make_lo(dve, n, n, in_width(n) if n < IN_CH else C)

        def three(pe, o, wh, wl, xh, xl, start, stop, w_moving):
            for t, (w, x) in enumerate(((wh, xh), (wh, xl), (wl, xh))):
                lhs, rhs = (x, w) if w_moving else (w, x)
                last = pe.matmul(o, lhs, rhs, start=start and t == 0, stop=stop and t == 2)
            return last

        def bc(ap, shape, axis):
            return ap.unsqueeze(axis).to_broadcast(shape)

        eye4 = bc(ident[:, :], [P, HP, P], 1)

        def tiles(ap, tt):
            return ap[:, :, ds(tt * P, P)]

        def tile_chunks(ap, tt):
            return ap.rearrange("p h (c t) -> p h c t", t=CH)[:, :, ds(tt * 2, 2), :]

        def of_level(ap, l, which):
            return ap.rearrange("p h (q w r) -> p h q w r", w=2, r=1 << l)[:, :, :, which, :]

        block = ctx.enter_context(nc.Block())

        @block.sync
        def _(sp):
            for tt in range(TT):
                sp.dma_start(H[:, tt, :], x_d[tt * P:(tt + 1) * P, :]).then_inc(S("x_in"), 16)
            for n in range(IN_CH):
                if n < 24:
                    g, q = n // 4, n % 4
                    ring.load(sp, n, n, w_in_v[:, 2 * q:2 * q + 2, 512 * g:512 * g + 512],
                               lambda r: r.rearrange("p (k n) -> p k n", k=2))
                else:
                    q = n - 24
                    ring.load(sp, n, n, w_in_v[:, 4 * q:4 * q + 4, 3072:3232],
                               lambda r: r[:, 0:640].rearrange("p (k n) -> p k n", k=4))
            for c in range(OUT_CH):
                ring.load(sp, IN_CH + c, IN_CH + c, w_out_v[:, c, :])
            sp.wait_ge(S("state_written"), 2 * TT + 1)
            sp.wait_ge(S("rwkv_out"), TT + 1)
            for tt in range(TT):
                sp.dma_start(H[:, tt, :], x_d[tt * P:(tt + 1) * P, :]).then_inc(S("x_in"), 16)
            sp.wait_ge(S("mix_added"), 8)
            sp.dma_start(g_ffn[:, :], t_in["norm_ffn_g"][0].partition_broadcast(P)).then_inc(S("g_ffn_in"), 16)
            for c in range(12):
                xring.load(sp, MOE0 + c, c, (wg_v if c < 8 else wu_v)[0, :, (c % 8) * C:(c % 8 + 1) * C])
            for tt in range(TT):
                sp.wait_ge(S("xn2_ok"), tt + 1)
                sp.dma_start(xn2_d[tt * P:(tt + 1) * P, :], XN2[:, tt, :]).then_inc(S("xn2_stored"), 16)

            def chunk_src(w, e, c):
                return w[ds(e, 1), :, c * C:(c + 1) * C].rearrange("o p n -> (o p) n")

            for c in range(12, 16):
                xring.load(sp, MOE0 + c, c, wu_v[0, :, (c % 8) * C:(c % 8 + 1) * C])
            sp.wait_ge(S("tables_ok"), 1)
            nb = sp.value_load(n_blk[0:1, 0:1], min_val=NE, max_val=NB - 1)
            last_blk = sp.value_load(n_blk[0:1, 1:2], min_val=NE - 1, max_val=NB - 2)

            def block_loads(i, final=False):
                first = isinstance(i, int) and i == 0
                e = sp.value_load(blk_exp[0:1, ds(i, 1)], min_val=0, max_val=NE - 1)
                base = MOE0 + 8 + i * PER
                work = [] if first else [(wu_v, e)]
                if not final:
                    work.append((wg_v, sp.value_load(blk_exp[0:1, ds(i + 1, 1)], min_val=0, max_val=NE - 1)))
                work.append((wd_v, e))
                for k, (w, ex) in enumerate(work, 1 if first else 0):
                    for c in range(8):
                        xring.load(sp, base + (8 * k + c), 8 + 8 * k + c, chunk_src(w, ex, c))

            block_loads(0)
            block_loads(1)
            with sp.Fori(0, (NB - 2) // 2) as it:
                for q in range(2):
                    i = it * 2 + (2 + q)
                    with sp.If(i < last_blk):
                        block_loads(i)
                    with sp.If(i == last_blk):
                        block_loads(i, final=True)
            sp.dma_start(g_fin[:, :], t_in["norm_final_g"].partition_broadcast(P)).then_inc(S("g_fin_in"), 16)
            sp.wait_ge(S("y_stored"), nb * 16)
            for tt in range(TT):
                if tt >= 2:
                    sp.wait_ge(S("combined"), tt - 1)
                rows = y_d[tt * P * TOPK:(tt + 1) * P * TOPK, :].rearrange("(p k) d -> p k d", k=TOPK)
                for f in range(2):
                    sp.dma_start(YG[:, tt % 2, 2 * f:2 * f + 2, :], rows[:, 2 * f:2 * f + 2, :])\
                        .then_inc(S(f"y_pairs_in{tt % 2}{f}"), 16)
            for tt in range(TT):
                sp.wait_ge(S("final_ok"), tt + 1)
                sp.dma_start(out[0, tt * P:(tt + 1) * P, :], FO[:, tt % 2, :]).then_inc(S("out_stored"), 16)
                if tt < TT - 2:
                    sp.wait_ge(S("out_stored"), 16 * (tt + 1))
                    sp.sem_inc(S("final_free"), 1)
            sp.wait_ge(S("out_stored"), 16 * TT)
            sp.wait_ge(S("xn2_stored"), 16 * TT)

        @block.gpsimd
        def _(pool):
            ch = Chain(pool, "pool_chain")
            pool.memset(par_rows[:, :], 0.0).then_inc(S("param_rows_zero"), 1)
            pool.memset(XR[:, :, 0:1], 0.0).then_inc(S("zero_columns"), 1)

            def keep(buf, view, pattern, base, cm, op, fill=0.0):
                ch.link(pool.affine_select(out=view, in_=view, compare_op=op, fill=fill, base=base,
                                           pattern=pattern, channel_multiplier=cm))

            ch.link(pool.memset(ident[:, :], 0.0))
            keep(ident, ident[:, :], [[-1, P]], 0, 1, ALU.not_equal, 1.0)
            pool.memset(neghalf[:, :], -0.5).then_inc(S("ident_ok"), 1)
            ch.link(pool.memset(head_ones[:, :], 0.0))
            ch.link(pool.memset(head_ones[0:64, 0:64], 1.0))
            ch.link(pool.memset(head_ones[64:128, 64:128], 1.0))
            ch.link(pool.tensor_copy(mask_su[:, :], head_ones[:, :]))
            ch.link(pool.tensor_copy(mask_iu[:, :], head_ones[:, :]))
            keep(mask_su, mask_su[:, :], [[1, P]], 0, -1, ALU.is_gt)
            keep(mask_iu, mask_iu[:, :], [[1, P]], 0, -1, ALU.is_ge)

            pool.wait_ge(S("ms_ok"), 1)
            pool.tensor_tensor(rms[:, 0:4], ss[:, 0:4], neghalf[:, :].to_broadcast([P, 4]), ALU.pow)\
                .then_inc(S("rms_ok"), 1)

            ch.link(pool.memset(lvl[:, :, :], 1.0))
            for l in range(6):
                b = 1 << l
                v = lvl[:, l, :].rearrange("p (q h r) -> p q h r", h=2, r=b)
                keep(lvl, v, [[-2 * b, P // (2 * b)], [-1000, 2], [0, b]], -b, 1, ALU.is_ge)
                keep(lvl, v, [[2 * b, P // (2 * b)], [0, 2], [0, b]], 2 * b - 1, -1, ALU.is_ge)
            ch.link(pool.memset(lvl0T[:, :], 1.0))
            keep(lvl0T, lvl0T[:, :].rearrange("p (q h) -> p q h", h=2), [[-2, 64], [-1000, 2]], 1000, 1, ALU.is_equal)
            ch.link(pool.iota(dist[:, :], [[1, 512]], base=-384, channel_multiplier=-1,
                              allow_small_or_imprecise_dtypes=True))
            keep(dist, dist[:, :], [[-1, 512]], 384, 1, ALU.is_ge, -1.0e30)
            ch.link(pool.memset(SCM[:, :], 1.0))
            pool.memset(SCM[:, :].rearrange("p (c t) -> p c t", t=CH + 1)[:, :, 0:1], 0.0)
            pool.memset(onesf[:, :], 1.0)
            ch.link(pool.memset(sel_T[:, :], 1.0))
            keep(sel_T, sel_T[:, :], [[1, 512]], 0, -HD, ALU.is_ge)
            keep(sel_T, sel_T[:, :], [[-1, 512]], HD - 1, HD, ALU.is_ge)
            pool.memset(ones_b[:, :], 1.0)
            pool.iota(iota32[:, :], [[1, NE]], base=0, channel_multiplier=0, allow_small_or_imprecise_dtypes=True)
            pool.iota(iotaB[:, :], [[1, NBT]], base=0, channel_multiplier=0, allow_small_or_imprecise_dtypes=True)
            pool.iota(iotaR[:, :], [[1, P]], base=0, channel_multiplier=0, allow_small_or_imprecise_dtypes=True)
            pool.iota(pair_ids[:, 0, :], [[0, 16]], base=0, channel_multiplier=4, allow_small_or_imprecise_dtypes=True)
            pool.iota(pair_ids[:, 1, :], [[512, 4], [0, 4]], base=0, channel_multiplier=0,
                      allow_small_or_imprecise_dtypes=True)
            ch.link(pool.iota(pair_ids[:, 2, :], [[0, 4], [1, 4]], base=1, channel_multiplier=0,
                              allow_small_or_imprecise_dtypes=True))
            for q in range(4):
                ch.link(pool.iota(lane32[32 * q:32 * q + 32, :], [[0, 1]], base=0, channel_multiplier=1,
                                  allow_small_or_imprecise_dtypes=True))
            ch.link(pool.memset(triu[:, :], 1.0))
            keep(triu, triu[:, :], [[1, P]], 0, -1, ALU.is_gt)
            pool.sem_inc(S("consts_ok"), 1)

            bias_src = [t_in[k][0] for k in ("moe_b_gate", "moe_b_up", "moe_b_down")]
            for w in range(3):
                for q in range(3):
                    pool.dma_start(bias_raw[32 * q:32 * q + 32, :], bias_src[w]).then_inc(S("bias_in"), 16)
                pool.wait_ge(S("bias_in"), 48 * (w + 1))
                for q in range(3):
                    lo, n = 32 * q, 96 - 32 * q
                    for r in range(lo, 96, 32):
                        ch.link(pool.tensor_copy(biasb[r:r + 32, w, :], bias_raw[r:r + 32, :]))
                    if q < 2:
                        for r in range(lo + 32, 96, 32):
                            ch.link(pool.tensor_tensor(bias_raw[r:r + 32, :], bias_raw[r:r + 32, :],
                                                       biasb[r:r + 32, w, :], ALU.subtract))

            pool.wait_ge(S("zero_columns"), 1)
            for i in range(14):
                rows = (64, 96)[i - 12] if i >= 12 else P
                pool.wait_ge(S("unshifted_ok"), i + 1)
                if i >= 2:
                    pool.wait_ge(S("shifted_ok"), i - 1)
                pool.tensor_tensor(DF[0:rows, i % 2, :], XR[0:rows, i % 2, 0:512], XR[0:rows, i % 2, 1:513],
                                   ALU.subtract).then_inc(S("diff_ok"), 1)

            for qt in range(TT):
                pool.wait_ge(S("att_ms"), qt + 1)
                pool.tensor_tensor(hrs[:, qt, :], hss[:, qt, :], neghalf[:, :].to_broadcast([P, 8]), ALU.pow)\
                    .then_inc(S("att_rms"), 1)

            pool.wait_ge(S("att_pv"), 16)
            pool.memset(SIG[:, :, :, 0:1], 0.0).then_inc(S("sig_zero"), 1)
            for h in range(HP):
                pool.wait_ge(S("sig_ok"), HP + h + 1)
                pool.wait_ge(S("kk_sq"), h + 1)
                ch.link(pool.tensor_scalar(T1[:, h % 2, :], AV[:, h, :], par[:, KA_ + h:KA_ + h + 1],
                                           one_m_ka[:, h:h + 1], ALU.mult, ALU.add))
                ch.link(pool.tensor_tensor(KX[:, h, :], KX[:, h, :], T1[:, h % 2, :], ALU.mult))
            pool.sem_inc(S("keys_ok"), 1)
            pool.wait_ge(S("att_done"), 1)
            pool.wait_ge(S("scans_ok"), 1)
            pool.memset(ST[:, :, :], 0.0).then_inc(S("state_written"), 1)
            RKP = par[:, RK_:RK_ + HP]
            lc = Chain(pool, "pool_tile_chain")

            def stage_keys(tt):
                pool.wait_ge(S("exp_ok"), tt * 2 + 2)
                pool.tensor_tensor(KSt[:, :, :].rearrange("p h (c t) -> p h c t", t=CH), tile_chunks(KX[:, :, :], tt),
                                   EI[:, :, :, :], ALU.mult)

            def stage_bonus(tt):
                lc.base, lc.n = tt * 1, 0
                lc.link(pool.tensor_tensor(BP[:, :, :], tiles(RX[:, :, :], tt), tiles(KX[:, :, :], tt), ALU.mult))
                pool.tensor_tensor(BP[:, :, :], BP[:, :, :], bc(RKP, [P, HP, P], 2), ALU.mult)\
                    .then_inc(S("bonus_prod"), 1)

            def stage_r(tt):
                pool.tensor_tensor(RSt[:, :, :].rearrange("p h (c t) -> p h c t", t=CH), tile_chunks(RX[:, :, :], tt),
                                   E01[:, :, :, 1:CH + 1], ALU.mult).then_inc(S("kr_tile"), 1)

            def add_identity(tt):
                pool.wait_ge(S("map_masked"), tt + 1)
                for c in range(2):
                    ins = pool.tensor_tensor(MTm[:, c], MTm[:, c], eye4, ALU.add)
                ins.then_inc(S("map_ok"), 1)

            stage_keys(0)
            stage_r(0)
            stage_bonus(0)
            with pool.Fori(0, TT - 1) as tt:
                pool.wait_ge(S("RK_ps"), tt + 1)
                stage_keys(tt + 1)
                pool.wait_ge(S("bonus_ps"), tt + 1)
                stage_bonus(tt + 1)
                add_identity(tt)
                pool.wait_ge(S("r2_ok"), tt + 1)
                stage_r(tt + 1)
            add_identity(TT - 1)

            for h in range(HP):
                pool.wait_ge(S("gn_sq"), h + 1)
                pool.wait_ge(S("gate_out"), h + 1)
                pool.tensor_tensor(RX[:, h, :], RX[:, h, :], GG[:, h, :], ALU.mult).then_inc(S("gn_scaled"), 1)

            pool.wait_ge(S("ms_ok"), 2)
            pool.tensor_tensor(rms[:, 4:8], ss[:, 4:8], neghalf[:, :].to_broadcast([P, 4]), ALU.pow)\
                .then_inc(S("rms_ok"), 1)

            last_x, last_y = pool.to_reg(SEQ - 1), pool.to_reg(SEQ * TOPK - 1)
            pool.wait_ge(S("xn2_stored"), 16 * TT)
            pool.wait_ge(S("x2T_ps"), TT)
            pool.memset(XB[:, :, :], 0.0).then_inc(S("xb_zero"), 1)
            pool.wait_ge(S("xb_zero"), 1)
            pool.wait_ge(S("slots_ok"), 1)
            ic = Chain(pool, "index_chain")

            def gather(j, q, links):
                ic.base, ic.n = links, 0
                ic.link(pool.tensor_copy(now_x[q][:, :], idx_x[:, ds(j, 1)]))
                pool.sem_inc(S("index_ready"), 1)
                pool.indirect_dma_start(
                    out=XB[:, q, :], out_offset=None, in_=xn2_d,
                    in_offset=bass.IndirectOffsetOnAxis(ap=now_x[q][:, :].bitcast(U32), axis=0),
                    bounds_check=last_x, oob_is_err=False).then_inc(S(f"xb_in{q}"), 16)

            def scatter(j, links):
                if not (isinstance(j, int) and j == 0):
                    pool.wait_ge(S("y_stored"), j * 16)
                ic.base, ic.n = links, 0
                ic.link(pool.tensor_copy(now_y[:, :], idx_y[:, ds(j, 1)]))
                pool.sem_inc(S("index_ready"), 1)
                pool.indirect_dma_start(
                    out=y_d, out_offset=bass.IndirectOffsetOnAxis(ap=now_y[:, :].bitcast(U32), axis=0),
                    in_=YB[:, :], in_offset=None,
                    bounds_check=last_y, oob_is_err=False).then_inc(S("y_stored"), 16)

            def select(j):
                pool.tensor_copy(bsel[:, :], expsel[:, ds(j, 1)].to_broadcast([96, P])).then_inc(S("bias_sel"), 1)

            gather(0, 0, 0)
            gather(1, 1, 1)
            pool.wait_ge(S("tables_ok"), 1)
            select(0)
            nb = pool.value_load(n_blk[0:1, 0:1], min_val=NE, max_val=NB - 1)
            last_blk = pool.value_load(n_blk[0:1, 1:2], min_val=NE - 1, max_val=NB - 2)

            def glu(i):
                pool.wait_ge(S("sigmoid_ok"), i + 1)
                pool.tensor_tensor(GT[:, :], GT[:, :], SG[:, :], ALU.mult).then_inc(S("glu_ok"), 1)

            def block_pool(i, q, prev):
                glu(i)
                pool.wait_ge(S("up_down_bias"), i + 1)
                pool.wait_ge(S("xT_ps"), i + 1)
                select(i + 1)
                gather(i + 2, q, 2 if prev is None else i * 2 + 1)
                if prev is not None:
                    pool.wait_ge(S("y_act"), i)
                    scatter(prev, i * 2 + 2)

            block_pool(0, 0, None)
            block_pool(1, 1, 0)
            with pool.Fori(0, (NB - 2) // 2) as it:
                for q in range(2):
                    i = it * 2 + (2 + q)
                    with pool.If(i < last_blk):
                        block_pool(i, q, it * 2 + (1 + q))
                    with pool.If(i == last_blk):
                        glu(i)
                        pool.wait_ge(S("y_act"), i)
                        scatter(it * 2 + (1 + q), i * 2 + 1)
            pool.wait_ge(S("y_act"), nb)
            scatter(last_blk, nb * 2)
            pool.wait_ge(S("y_stored"), nb * 16)
            pool.wait_ge(S("xb_in0"), (nb + 2) // 2 * 16)
            pool.wait_ge(S("xb_in1"), (nb + 1) // 2 * 16)
            for tt in range(TT):
                pool.wait_ge(S("ms_ok"), tt + 3)
                pool.tensor_tensor(rms[:, 8 + tt:9 + tt], ss[:, 8 + tt:9 + tt], neghalf[:, :], ALU.pow)\
                    .then_inc(S("rms_ok"), 1)

        def xT_hi(act, j, q):
            act.wait_ge(S("xT_ps"), j + 1)
            for b in range(2):
                ins = act.activation(xbh[q][:, 4 * b:4 * b + 4, :].rearrange("p k t -> p (k t)"), bank[6 + b], ACT.Copy)
            ins.then_inc(S("xT_hi"), 1)

        def y_act(act, i, prev, short=0):
            act.wait_ge(w_used, i * PER + (MOE0 + 8 - short))
            if not (isinstance(prev, int) and prev == 0):
                act.wait_ge(S("y_stored"), prev * 16)
            act.activation(YB[:, :], pair[2][:, :], ACT.Copy).then_inc(S("y_act"), 1)

        def block_act(act, i, q, prev, final=False):
            base = MOE0 + 8 + i * PER

            def hi(k):
                xring.make_hi(act, base + k, 8 + k, i * (PER // NRAW2) + (8 + k) // NRAW2)

            for k in range(2):
                hi(k)
            act.wait_ge(S("gate_ok"), i + 1)
            act.activation(SG[:, :], GT[:, :], ACT.Sigmoid, scale=ALPHA).then_inc(S("sigmoid_ok"), 1)
            for k in range(2, 4):
                hi(k)
            if prev is not None:
                y_act(act, i, prev)
            for k in range(4, 8):
                hi(k)
            if not final:
                xT_hi(act, i + 1, 1 - q)
            for k in range(8, 11 if final else 17):
                hi(k)
            act.wait_ge(S("hT_ps"), i + 1)
            for b in range(2):
                ins = act.activation(hbh[:, 4 * b:4 * b + 4, :].rearrange("p k t -> p (k t)"), bank[6 + b], ACT.Copy)
            ins.then_inc(S("hT_hi"), 1)
            for k in range(11, 16) if final else range(17, 24):
                hi(k)

        @block.scalar
        def _(act):
            act.dma_start(g_mix[:, :], t_in["norm_mix_g"][0].rearrange("(p k) -> p k", k=KT)).then_inc(S("params_in"), 16)

            act.wait_ge(S("x_in"), 64)
            for tt in range(TT):
                ins = act.activation(pair[tt][:, :], H[:, tt, :], ACT.Square, accum_out=ss[:, tt:tt + 1])
            ins.then_inc(S("squares_ok"), 1)
            act.dma_start(w2a2[0:32, :], t_in["rwkv_w2"][0]).then_inc(S("params_in"), 16)
            act.dma_start(w2a2[32:64, :], t_in["rwkv_a2"][0]).then_inc(S("params_in"), 16)
            act.dma_start(g2[:, :], t_in["rwkv_g2"][0]).then_inc(S("params_in"), 16)
            act.dma_start(w_rout[:, :, :], t_in["w_router"][0].rearrange("(p k) e -> p k e", k=KT))\
                .then_inc(S("params_in"), 16)
            act.dma_start(b_rout[:, :], t_in["b_router"][0].partition_broadcast(P)).then_inc(S("params_in"), 16)
            act.wait_ge(S("param_rows_zero"), 1)
            mu = t_in["rwkv_mu"][0]
            act.dma_start(par_rows[MU:MU + 12, :], mu[0:1536].rearrange("(r c) -> r c", c=P)).then_inc(S("params_in"), 16)
            act.dma_start(par_rows[MU + 12:MU + 13, 0:64], mu[1536:1600].unsqueeze(0)).then_inc(S("params_in"), 16)
            act.dma_start(par_rows[MU + 13:MU + 14, 0:96], mu[1600:1696].unsqueeze(0)).then_inc(S("params_in"), 16)
            for row, name in ((W0, "rwkv_w0"), (A0, "rwkv_a0"), (KK_, "rwkv_k_k"), (KA_, "rwkv_k_a"),
                              (LNG, "rwkv_ln_g"), (LNB, "rwkv_ln_b"), (ATG, "attn_norm_g")):
                act.dma_start(par_rows[row:row + 4, :], t_in[name][0].rearrange("(r c) -> r c", c=P))\
                    .then_inc(S("params_in"), 16)
            act.dma_start(par_rows[RK_:RK_ + 4, :], t_in["rwkv_r_k"][0].rearrange("(r a) c -> r (a c)", a=2))\
                .then_inc(S("params_in"), 16)
            hi_range(act, 0, 4)
            act.wait_ge(S("params_in"), 16 * NPAR)
            act.wait_ge(S("xT_first"), TT)
            for k in range(KT):
                act.activation(xnh[:, k, :], bank[k], ACT.Copy, scale=g_mix[:, k:k + 1]).then_inc(S("xnh_ok"), 1)

            for g in range(7):
                b0 = (g % 2) * 4
                hi_range(act, 4 * g + 4, min(4 * g + 8, IN_CH + NHL))
                act.wait_ge(w_used, min(4 * g + 4, IN_CH))
                if g == 0:
                    for c in range(4):
                        ins = act.activation(QT[:, c, :], bank[b0 + c], ACT.Copy, scale=HD ** -0.5)
                    ins.then_inc(S("qv_out"), 1)
                elif g == 2:
                    for c in range(4):
                        ins = act.activation(VA[:, c, :], bank[b0 + c], ACT.Copy)
                    ins.then_inc(S("qv_out"), 1)
                elif g >= 3:
                    for c in range(4 if g < 6 else 2):
                        i = 4 * (g - 3) + c
                        rows = P if g < 6 else (64, 96)[c]
                        if i >= 2:
                            act.wait_ge(S("shifted_ok"), i - 1)
                        act.activation(XR[0:rows, i % 2, 1:513], bank[b0 + c][0:rows, :], ACT.Copy)\
                            .then_inc(S("unshifted_ok"), 1)

            for u in range(17):
                if u < 16:
                    nk, z = (u // 4 + 1) * P, u % 2
                    act.wait_ge(S("scores_ok"), u + 1)
                    if u >= 2:
                        act.wait_ge(S("probsT_ps"), u - 1)
                    for j in range(2):
                        ins = act.activation(PR[:, z, j, 0:nk], SC[:, z, j, 0:nk], ACT.Exp,
                                             bias=nmax[:, 2 * u + j:2 * u + j + 1],
                                             accum_out=rsum[:, 2 * u + j:2 * u + j + 1])
                    ins.then_inc(S("probs_ok"), 1)
                if u >= 1:
                    v = u - 1
                    nk = (v // 4 + 1) * P
                    act.wait_ge(S("probsT_ps"), v + 1)
                    if v >= 2:
                        act.wait_ge(S("att_pv"), v - 1)
                    act.activation(PRT[:, v % 2, :, 0:nk], pair[2][:, :].rearrange("p (j k) -> p j k", j=2)[:, :, 0:nk],
                                   ACT.Copy).then_inc(S("probsT_ok"), 1)

            act.wait_ge(S("att_pv"), 16)
            act.activation(TL[:, :], XL[0:32, 0, :], ACT.Tanh)
            act.activation(XL[0:96, 1, :], XL[0:96, 1, :], ACT.Sigmoid).then_inc(S("lora_in"), 1)
            for h in range(HP):
                act.activation(KKN[:, h, :], KX[:, h, :], ACT.Copy, scale=n_k_k[:, h:h + 1])
                act.activation(T4[:, h, :], KX[:, h, :], ACT.Square, scale=n_k_k[:, h:h + 1])\
                    .then_inc(S("kk_sq"), 1)
            act.wait_ge(S("sig_zero"), 1)
            for h in range(HP):
                act.wait_ge(S("lora_ps"), h + 1)
                act.activation(SIG[:, h, :, 1:CH + 1], bank[h].rearrange("p (c t) -> p c t", t=CH), ACT.Sigmoid,
                               bias=par[:, W0 + h:W0 + h + 1]).then_inc(S("sig_ok"), 1)
            def norm_root(n):
                act.wait_ge(S("norm_in"), n + 1)
                act.activation(NR[:, :], NV[:, :], ACT.Sqrt).then_inc(S("norm_root"), 1)

            def norm_rows(n, b):
                act.wait_ge(S("normT_ps"), n + 1)
                act.activation((NRT0, NRT1)[n][:, :], bank[b][0:8, :], ACT.Copy).then_inc(S("normT_ok"), 1)

            norm_root(0)
            act.wait_ge(S("att_done"), 1)
            for h in range(HP):
                act.wait_ge(S("lora_ps"), HP + h + 1)
                act.activation(AV[:, h, :], bank[4 + h], ACT.Sigmoid, bias=par[:, A0 + h:A0 + h + 1])\
                    .then_inc(S("sig_ok"), 1)

            norm_rows(0, 1)
            act.sem_inc(S("rwkv_out"), 1)

            def stage_act(tt):
                cs = CS[:, :, ds(tt * 2, 2), :]
                act.activation(E01[:, :, :, :], cs, ACT.Exp, scale=-DECAY).then_inc(S("exp_ok"), 1)
                act.activation(EI[:, :, :, :], cs[:, :, :, 1:CH + 1], ACT.Exp, scale=DECAY).then_inc(S("exp_ok"), 1)
                act.activation(VSt[:, :, :], tiles(VX[:, :, :], tt), ACT.Copy).then_inc(S("v_tile"), 1)

            def tile_act(tt, stage_next):
                act.wait_ge(S("rows_ps"), tt + 1)
                act.activation(Bt[:, :], bank[1], ACT.Copy)
                act.activation(Kt[:, :], bank[2], ACT.Copy)
                act.activation(Vt[:, :], bank[3], ACT.Copy).then_inc(S("bkv_rows"), 1)
                act.wait_ge(S("AT_ps"), tt + 1)
                for j in range(2):
                    ins = act.activation(AsT[:, j].rearrange("p h t -> p (h t)"), bank[4 + j], ACT.Copy)
                ins.then_inc(S("AT_ok"), 1)
                if stage_next:
                    act.wait_ge(S("a_rows"), tt + 1)
                    act.wait_ge(S("ab_tile"), tt + 1)
                    act.wait_ge(S("kr_tile"), tt + 1)
                    stage_act(tt + 1)
                act.wait_ge(S("z0_ps"), tt + 1)
                act.activation(AZ[:, :, 1, :], bank[6].rearrange("p (h d) -> p h d", d=CH), ACT.Copy)\
                    .then_inc(S("z0_rows"), 1)
                act.wait_ge(S("uz_ps"), tt + 1)
                uz = UZ[:, :, :, :].rearrange("p c (h j) d -> p j h c d", j=2)
                for j in range(2):
                    ins = act.activation(uz[:, j], bank[6 + j].rearrange("p (h c d) -> p h c d", h=HP, c=2), ACT.Copy)
                ins.then_inc(S("uz_rows"), 1)
                act.wait_ge(S("out_ps"), tt + 1)
                act.activation(tiles(RX[:, :, :], tt), bank[5].rearrange("p (h t) -> p h t", t=P), ACT.Copy)\
                    .then_inc(S("rwkv_out"), 1)

            act.wait_ge(S("scans_ok"), 1)
            act.wait_ge(S("norm_ps"), 1)
            stage_act(0)
            with act.Fori(0, TT - 1) as tt:
                tile_act(tt, True)
            tile_act(TT - 1, False)

            act.wait_ge(S("state_written"), 2 * TT + 1)
            for h in range(HP):
                act.wait_ge(S("gn_centered"), h + 1)
                act.activation(U2[:, h, :], RX[:, h, :], ACT.Square).then_inc(S("gn_sq"), 1)

            def gate(h):
                act.wait_ge(S("gate_ps"), h + 1)
                act.activation(G[:, h, :], bank[h], ACT.Copy)
                act.activation(GG[:, h, :], bank[h], ACT.Copy, scale=par[:, LNG + h:LNG + h + 1])\
                    .then_inc(S("gate_out"), 1)

            for h in range(2):
                gate(h)
            norm_root(1)
            gate(2)
            norm_rows(1, 5)
            gate(3)
            for c in range(4):
                act.activation(mxh[:, c, :], MA[:, c, :], ACT.Copy).then_inc(S("mix_hi_ok"), 1)
            for h in range(HP):
                act.wait_ge(S("gn_normed"), h + 1)
                act.activation(mxh[:, 4 + h, :], RX[:, h, :], ACT.Copy).then_inc(S("mix_hi_ok"), 1)
            hi_range(act, IN_CH + NHL, MOE0)
            for tt in range(TT):
                act.wait_ge(S("mix_added"), 2 * tt + 2)
                ins = act.activation(pair[tt][:, :], H[:, tt, :], ACT.Square, accum_out=ss[:, 4 + tt:5 + tt])
            ins.then_inc(S("squares_ok"), 1)
            for c in range(4):
                xring.make_hi(act, MOE0 + c, c, c // NRAW2)
            act.wait_ge(S("x2T_ps"), TT)
            for k in range(0, KT, 2):
                act.activation(X2T[:, k, :], bank[k], ACT.Copy).then_inc(S("x2T_act"), 1)
            for c in range(4, 8):
                xring.make_hi(act, MOE0 + c, c, c // NRAW2)
            act.wait_ge(S("top_ok"), 1)
            for tt in range(TT):
                ins = act.activation(gates[:, tt, :], top8[:, tt, 0:4], ACT.Exp, bias=ntop[:, tt:tt + 1],
                                     accum_out=gsum[:, tt:tt + 1])
            ins.then_inc(S("gate_exp"), 1)

            xT_hi(act, 0, 0)
            act.wait_ge(S("tables_ok"), 1)
            nb = act.value_load(n_blk[0:1, 0:1], min_val=NE, max_val=NB - 1)
            last_blk = act.value_load(n_blk[0:1, 1:2], min_val=NE - 1, max_val=NB - 2)
            block_act(act, 0, 0, None)
            block_act(act, 1, 1, 0)
            with act.Fori(0, (NB - 2) // 2) as it:
                for q in range(2):
                    i = it * 2 + (2 + q)
                    with act.If(i < last_blk):
                        block_act(act, i, q, it * 2 + (1 + q))
                    with act.If(i == last_blk):
                        block_act(act, i, q, it * 2 + (1 + q), final=True)
            y_act(act, nb, last_blk, 8)
            for tt in range(TT):
                act.wait_ge(S("combined"), tt + 1)
                act.activation(pair[tt][:, :], H[:, tt, :], ACT.Square,
                               accum_out=ss[:, 8 + tt:9 + tt]).then_inc(S("squares_ok"), 1)


        def xT_lo(dve, j, q):
            dve.wait_ge(S("xT_hi"), j + 1)
            for b in range(2):
                ins = dve.tensor_tensor(xbl[q][:, 4 * b:4 * b + 4, :].rearrange("p k t -> p (k t)"), bank[6 + b],
                                        xbh[q][:, 4 * b:4 * b + 4, :].rearrange("p k t -> p (k t)").bitcast(F32),
                                        ALU.subtract)
            ins.then_inc(S("xT_ok"), 1)

        def gate_part(dve, j):
            if isinstance(j, int) and j == 0:
                dve.wait_ge(w_used, MOE0 + 8)
            else:
                dve.wait_ge(w_used, j * PER + MOE0)
                dve.wait_ge(S("h_ok"), j)
            dve.tensor_scalar(GT[:, :], pair[0][:, :], LIMIT, None, ALU.min).then_inc(S("gate_ok"), 1)

        def block_dve(dve, i, q, final=False):
            base = MOE0 + 8 + i * PER

            def lo(k):
                xring.make_lo(dve, base + k, 8 + k)

            for k in range(8):
                lo(k)
            if not final:
                xT_lo(dve, i + 1, 1 - q)
            for k in range(8, 10 if final else 12):
                lo(k)
            dve.wait_ge(w_used, base + 8)
            dve.tensor_scalar(UP[:, :], pair[1][:, :], LIMIT, -LIMIT, ALU.min, ALU.max).then_inc(S("up_ok"), 1)
            dve.wait_ge(S("up_ok"), i + 1)
            dve.wait_ge(S("glu_ok"), i + 1)
            dve.scalar_tensor_tensor(HB[:, :], UP[:, :], 1.0, GT[:, :], ALU.add, ALU.mult).then_inc(S("h_ok"), 1)
            for k in range(10, 11) if final else range(12, 17):
                lo(k)
            dve.wait_ge(S("hT_hi"), i + 1)
            for b in range(2):
                ins = dve.tensor_tensor(hbl[:, 4 * b:4 * b + 4, :].rearrange("p k t -> p (k t)"), bank[6 + b],
                                        hbh[:, 4 * b:4 * b + 4, :].rearrange("p k t -> p (k t)").bitcast(F32),
                                        ALU.subtract)
            ins.then_inc(S("hT_ok"), 1)
            if final:
                for k in range(11, 16):
                    lo(k)
            else:
                for k in range(17, 20):
                    lo(k)
                gate_part(dve, i + 1)
                for k in range(20, 24):
                    lo(k)

        @block.vector
        def _(dve):
            ch = Chain(dve, "dve_chain")
            dve.wait_ge(S("squares_ok"), 1)
            dve.tensor_scalar(ss[:, 0:4], ss[:, 0:4], 1.0 / D, EPS, ALU.mult, ALU.add).then_inc(S("ms_ok"), 1)
            dve.wait_ge(S("rms_ok"), 1)
            for tt in range(TT):
                if tt >= 2:
                    dve.wait_ge(S("xT_first"), tt - 1)
                dve.tensor_scalar(xs[:, tt % 2, :], H[:, tt, :], rms[:, tt:tt + 1], None, ALU.mult).then_inc(S("xs_ok"), 1)
            lo_range(dve, 0, 4)
            for k in range(KT):
                dve.wait_ge(S("xnh_ok"), k + 1)
                dve.scalar_tensor_tensor(xnl[:, k, :], bank[k], g_mix[:, k:k + 1], xnh[:, k, :].bitcast(F32),
                                         ALU.mult, ALU.subtract).then_inc(S("xnl_ok"), 1)

            dve.wait_ge(S("param_ps"), 1)
            ch.link(dve.tensor_copy(par[:, :], bank[7][:, 0:48]))
            dve.tensor_scalar(n_k_k[:, :], par[:, KK_:KK_ + 4], -1.0, None, ALU.mult)
            dve.tensor_scalar(one_m_ka[:, :], par[:, KA_:KA_ + 4], -1.0, 1.0, ALU.mult, ALU.add).then_inc(S("params_ok"), 1)

            dsts = [RX, KX, VX]
            for g in range(7):
                b0 = (g % 2) * 4
                lo_range(dve, 4 * g + 4, min(4 * g + 8, IN_CH + NHL))
                if g == 1:
                    dve.wait_ge(w_used, 8)
                    for c in range(4):
                        ins = dve.tensor_copy(KTT[:, c, :], bank[b0 + c])
                    ins.then_inc(S("group1_out"), 1)
                elif g >= 3:
                    for c in range(4 if g < 6 else 2):
                        i = 4 * (g - 3) + c
                        rows = P if g < 6 else (64, 96)[c]
                        dst = dsts[g - 3][:, c, :] if g < 6 else XL[0:rows, c, :]
                        dve.wait_ge(S("diff_ok"), i + 1)
                        dve.scalar_tensor_tensor(dst, DF[0:rows, i % 2, :], par[0:rows, MU + i:MU + i + 1],
                                                 XR[0:rows, i % 2, 1:513], ALU.mult, ALU.add)\
                            .then_inc(S("shifted_ok"), 1)

            def finish_queries(qt):
                b = bank[6 + qt % 2].rearrange("p (h d) -> p h d", d=HD)
                dve.wait_ge(S("att_pv"), 4 * (qt + 1))
                if qt:
                    dve.wait_ge(S("attT_ps"), qt)
                ch.link(dve.reciprocal(rinv[:, 8 * qt:8 * qt + 8], rsum[:, 8 * qt:8 * qt + 8]))
                ch.link(dve.tensor_tensor(ON[:, :, :], b, bc(rinv[:, 8 * qt:8 * qt + 8], [P, 8, HD], 2), ALU.mult))
                ch.link(dve.tensor_tensor(OSQ[:, :, :], ON[:, :, :], ON[:, :, :], ALU.mult))
                ch.link(dve.reduce_sum(hss[:, qt, :], OSQ[:, :, :], AXX))
                dve.tensor_scalar(hss[:, qt, :], hss[:, qt, :], 1.0 / HD, EPS, ALU.mult, ALU.add).then_inc(S("att_ms"), 1)
                dve.wait_ge(S("att_rms"), qt + 1)
                dve.tensor_tensor(ON[:, :, :], ON[:, :, :], bc(hrs[:, qt, :], [P, 8, HD], 2), ALU.mult)\
                    .then_inc(S("att_on"), 1)

            def gain(qt):
                dve.wait_ge(S("attT_ps"), qt + 1)
                return dve.tensor_tensor(MA[:, :, qt * P:(qt + 1) * P], bank[4].rearrange("p (c t) -> p c t", t=P),
                                         bc(par[:, ATG:ATG + 4], [P, 4, P], 2), ALU.mult)

            dve.wait_ge(S("consts_ok"), 1)
            for u in range(16):
                nk, z = (u // 4 + 1) * P, u % 2
                dve.wait_ge(S("scores_ps"), u + 1)
                if u >= 2:
                    dve.wait_ge(S("probs_ok"), u - 1)
                for j in range(2):
                    ins = dve.scalar_tensor_tensor(SC[:, z, j, 0:nk], dist[:, 512 - nk:512], 2.0 ** -(2 * (u % 4) + j + 1),
                                                   bank[2 * z + j][:, 0:nk], ALU.mult, ALU.add)
                ch.link(ins)
                dve.reduce_max(nmax[:, 2 * u:2 * u + 2], SC[:, z, :, 0:nk], AXX, negate=True).then_inc(S("scores_ok"), 1)
                if u % 4 == 3 and u > 4:
                    finish_queries(u // 4 - 1)
                    gain(u // 4 - 1).then_inc(S("att_gained"), 1)
            finish_queries(3)
            gain(3).then_inc(S("att_gained"), 1)
            dve.wait_ge(S("att_gained"), 4)
            dve.wait_ge(S("probsT_ok"), 16)
            dve.sem_inc(S("att_done"), 1)

            def inverse_root(y, x, tmp):
                ch.link(dve.reciprocal(y, y))
                ch.link(dve.tensor_tensor(tmp, y, y, ALU.mult))
                ch.link(dve.scalar_tensor_tensor(tmp, tmp, -0.5, x, ALU.mult, ALU.mult))
                ch.link(dve.scalar_tensor_tensor(y, tmp, 1.5, y, ALU.add, ALU.mult))

            def scan(h):
                dve.wait_ge(S("sig_ok"), h + 1)
                return dve.tensor_tensor_scan(CS[:, h, :, :].rearrange("p c t -> p (c t)"), SCM[:, :],
                                              SIG[:, h, :, :].rearrange("p c t -> p (c t)"), 0.0, ALU.mult, ALU.add)

            dve.wait_ge(S("norm_ps"), 1)
            dve.tensor_scalar(NV[:, :], bank[5][:, 0:8 * TT], 1e-24, None, ALU.max).then_inc(S("norm_in"), 1)
            dve.wait_ge(S("sig_zero"), 1)
            scan(0)
            scan(1)
            dve.wait_ge(S("norm_root"), 1)
            inverse_root(NR[:, :], NV[:, :], NT[:, :])
            dve.sem_inc(S("norm_inv"), 1)
            scan(2)
            scan(3).then_inc(S("scans_ok"), 1)
            for h in range(HP):
                dve.wait_ge(S("norm_bc"), h + 1)
                ch.link(dve.tensor_tensor(KKN[:, h, :], KKN[:, h, :], bank[h], ALU.mult))
                dve.wait_ge(S("sig_ok"), HP + h + 1)
                ins = dve.scalar_tensor_tensor(BV[:, h, :], KKN[:, h, :], -1.0, AV[:, h, :], ALU.mult, ALU.mult)
            ch.link(ins)
            dve.wait_ge(S("keys_ok"), 1)
            dve.sem_inc(S("prep_done"), 1)

            def m4(m):
                return bc(m, [P, HP, P], 1)

            def bk(b):
                return bank[b].rearrange("p (h t) -> p h t", t=P)

            lc = Chain(dve, "dve_tile_chain")
            DVE_LINKS = 5
            def stage_ab(tt):
                dve.wait_ge(S("exp_ok"), tt * 2 + 2)
                dve.tensor_tensor(ASt[:, :, :].rearrange("p h (c t) -> p h c t", t=CH), tile_chunks(KKN[:, :, :], tt),
                                  E01[:, :, :, 0:CH], ALU.mult)
                dve.tensor_tensor(BSt[:, :, :].rearrange("p h (c t) -> p h c t", t=CH), tile_chunks(BV[:, :, :], tt),
                                  EI[:, :, :, :], ALU.mult).then_inc(S("ab_tile"), 1)

            def tile_dve(tt, stage_next):
                lc.base, lc.n = tt * DVE_LINKS, 0
                dve.wait_ge(S("state_written"), tt * 2 + 1)
                lc.link(dve.tensor_copy(DEC[:, :, :, :], E01[:, :, :, CH:CH + 1]))
                dve.wait_ge(S("rows_ps"), tt + 1)
                dve.tensor_copy(AZ[:, :, 0, :], bank[0].rearrange("p (h d) -> p h d", d=CH)).then_inc(S("a_rows"), 1)
                dve.wait_ge(S("AT_ps"), tt + 1)
                for j in range(2):
                    dve.tensor_tensor(Xi[:, j], bk(6 + j), m4(lvl[:, 0, :]), ALU.mult)
                dve.wait_ge(S("AT_ok"), tt + 1)
                for j in range(2):
                    ins = dve.tensor_tensor(XiT[:, j], bk(4 + j), m4(lvl0T[:, :]), ALU.mult)
                lc.link(ins)
                for j in range(2):
                    dve.tensor_tensor(XiT[:, j], XiT[:, j], eye4, ALU.add)
                    dve.tensor_tensor(Xi[:, j], Xi[:, j], eye4, ALU.add).then_inc(S("inv_ok"), 1)
                dve.wait_ge(S("TK_ps"), tt + 1)
                for j in range(2):
                    ins = dve.tensor_tensor(TKm[:, j], bk(j), m4(mask_su[:, :]), ALU.mult)
                ins.then_inc(S("TK_ok"), 1)
                for j in range(2):
                    ins = dve.tensor_tensor(RBm[:, j], bk(2 + j), m4(mask_iu[:, :]), ALU.mult)
                ins.then_inc(S("RB_ok"), 1)
                dve.wait_ge(S("RK_ps"), tt + 1)
                for j in range(2):
                    ins = dve.tensor_tensor(RKm[:, j], bk(4 + j), m4(mask_iu[:, :]), ALU.mult)
                ins.then_inc(S("RK_ok"), 1)
                vt = tiles(VX[:, :, :], tt)
                dve.wait_ge(S("v_tile"), tt + 1)
                dve.wait_ge(S("bonus_ps"), tt + 1)
                dve.tensor_tensor(vt, bk(6), vt, ALU.mult).then_inc(S("bonus_ok"), 1)
                for l in range(1, 6):
                    for j in range(2):
                        dve.wait_ge(S("step_ps"), tt * 10 + (2 * (l - 1) + j + 1))
                        dve.tensor_tensor(Pm[:, j], bk(j), m4(lvl[:, l, :]), ALU.mult).then_inc(S("step_ok"), 1)
                    for j in range(2):
                        dve.wait_ge(S("inv_ps"), tt * 10 + (2 * (l - 1) + j + 1))
                        if l < 5:
                            xi = of_level(Xi[:, j], l, 0)
                            dve.tensor_tensor(xi, xi, of_level(bk(2 + j), l, 0), ALU.add)
                        xt = of_level(XiT[:, j], l, 1)
                        dve.tensor_tensor(xt, xt, of_level(bk(4 + j), l, 1), ALU.add).then_inc(S("inv_ok"), 1)
                if stage_next:
                    stage_ab(tt + 1)
                dve.wait_ge(S("map_ps"), tt + 1)
                for c in range(2):
                    ins = dve.tensor_tensor(MTm[:, c], bk(1 + c), m4(head_ones[:, :]), ALU.mult)
                ins.then_inc(S("map_masked"), 1)
                dve.wait_ge(S("r2_ps"), tt + 1)
                dve.tensor_tensor(R2[:, :, :], bk(0), RSt[:, :, :], ALU.add).then_inc(S("r2_ok"), 1)
                dve.wait_ge(S("add_ps"), tt + 1)
                for c in range(2):
                    ins = dve.tensor_tensor(NN[:, c], bk(3 + c), m4(head_ones[:, :]), ALU.mult)
                lc.link(ins)
                for c in range(2):
                    dve.wait_ge(S("chain_ps"), tt * 2 + (c + 1))
                    lc.link(dve.tensor_tensor(SN[:, :, :], bk(6 + c), NN[:, c], ALU.add))
                    dve.tensor_tensor(ST[:, :, :], SN[:, :, :],
                                      DEC[:, :, c, :].to_broadcast([P, HP, P]), ALU.mult)\
                        .then_inc(S("state_written"), 1)
                assert lc.n == DVE_LINKS

            stage_ab(0)
            with dve.Fori(0, TT - 1) as tt:
                tile_dve(tt, True)
            tile_dve(TT - 1, False)

            dve.wait_ge(S("rwkv_out"), TT + 1)
            for h in range(HP):
                dve.wait_ge(S("gn_mean"), h + 1)
                dve.scalar_tensor_tensor(RX[:, h, :], bank[4 + h], -1.0 / HD, RX[:, h, :], ALU.mult, ALU.add)\
                    .then_inc(S("gn_centered"), 1)

            def gated_bonus(h):
                dve.wait_ge(S("gate_out"), h + 1)
                dve.scalar_tensor_tensor(VX[:, h, :], VX[:, h, :], par[:, LNB + h:LNB + h + 1], G[:, h, :],
                                         ALU.add, ALU.mult).then_inc(S("bonus_gated"), 1)

            def mix_low(c, src):
                dve.wait_ge(S("mix_hi_ok"), c + 1)
                dve.tensor_tensor(mxl[:, c, :], src, mxh[:, c, :].bitcast(F32), ALU.subtract).then_inc(S("mix_ok"), 1)

            gated_bonus(0)
            dve.wait_ge(S("norm_ps"), 2)
            dve.tensor_scalar(NV[:, :], bank[4][:, 0:8 * TT], 1.0 / HD, GN_EPS, ALU.mult, ALU.add)\
                .then_inc(S("norm_in"), 1)
            gated_bonus(1)
            dve.wait_ge(S("norm_root"), 2)
            inverse_root(NR[:, :], NV[:, :], NT[:, :])
            dve.sem_inc(S("norm_inv"), 1)
            gated_bonus(2)
            gated_bonus(3)
            for h in range(HP):
                dve.wait_ge(S("norm_bc"), HP + h + 1)
                dve.wait_ge(S("gn_scaled"), h + 1)
                ch.link(dve.tensor_tensor(RX[:, h, :], RX[:, h, :], bank[4 + h], ALU.mult))
                dve.wait_ge(S("bonus_gated"), h + 1)
                dve.tensor_tensor(RX[:, h, :], RX[:, h, :], VX[:, h, :], ALU.add).then_inc(S("gn_normed"), 1)
            for c in range(4):
                mix_low(c, MA[:, c, :])
            for h in range(HP):
                mix_low(4 + h, RX[:, h, :])
            lo_range(dve, IN_CH + NHL, MOE0)
            dve.wait_ge(S("x_in"), 128)
            dve.wait_ge(w_used, MOE0)
            for tt in range(TT):
                for f in range(2):
                    hs = H[:, tt, 512 * f:512 * f + 512]
                    dve.tensor_tensor(hs, hs, bank[2 * tt + f], ALU.add).then_inc(S("mix_added"), 1)

            dve.wait_ge(S("squares_ok"), 2)
            dve.tensor_scalar(ss[:, 4:8], ss[:, 4:8], 1.0 / D, EPS, ALU.mult, ALU.add).then_inc(S("ms_ok"), 1)
            dve.wait_ge(S("g_ffn_in"), 16)
            dve.wait_ge(S("rms_ok"), 2)
            for tt in range(TT):
                dve.scalar_tensor_tensor(XN2[:, tt, :], H[:, tt, :], rms[:, 4 + tt:5 + tt], g_ffn[:, :],
                                         ALU.mult, ALU.mult).then_inc(S("xn2_ok"), 1)
            for c in range(2):
                xring.make_lo(dve, MOE0 + c, c)
            dve.wait_ge(S("x2T_ps"), TT)
            for k in range(1, KT, 2):
                dve.tensor_copy(X2T[:, k, :], bank[k]).then_inc(S("x2T_dve"), 1)
            for c in range(2, 6):
                xring.make_lo(dve, MOE0 + c, c)

            dve.wait_ge(S("logits_ps"), 1)
            ch.link(dve.tensor_tensor(LG[:, :, :], bank[0][:, 0:128].rearrange("p (t e) -> p t e", e=NE),
                                      bc(b_rout[:, :], [P, TT, NE], 1), ALU.add))
            for tt in range(TT):
                ins = dve.max(top8[:, tt, :], LG[:, tt, :])
            ch.link(ins)
            for tt in range(TT):
                dve.max_index(idx8[:, tt, :], top8[:, tt, :], LG[:, tt, :])
            ins = dve.tensor_scalar(ntop[:, :], top8[:, :, 0], -1.0, None, ALU.mult)
            ch.link(ins)
            dve.sem_inc(S("top_ok"), 1)
            ch.link(dve.tensor_copy(idx8f[:, :, :], idx8[:, :, :]))
            ch.link(dve.tensor_tensor(OH[:, :, :, :], idx8f[:, :, 0:4].unsqueeze(3).to_broadcast([P, TT, TOPK, NE]),
                                      iota32[:, :].unsqueeze(1).unsqueeze(1).to_broadcast([P, TT, TOPK, NE]), ALU.is_equal))
            with nc.allow_low_precision("memberships are 0 or 1"):
                dve.reduce_sum(MB[:, :, :], OH[:, :, :, :].rearrange("p t k e -> p t e k"), AXX).then_inc(S("member_ok"), 1)
            dve.wait_ge(S("gate_exp"), 1)
            ch.link(dve.reciprocal(rgs[:, :], gsum[:, :]))
            ch.link(dve.tensor_tensor(gates[:, :, :], gates[:, :, :], bc(rgs[:, :], [P, TT, TOPK], 2), ALU.mult))

            dve.wait_ge(S("rank_ps"), 1)
            cnt = bank[2][:, 0:NE]
            for b in range(4):
                ins = dve.tensor_scalar(nbv[:, b, :], cnt, float(P * b) if b else -1.0, None, ALU.is_gt)
            ch.link(ins)
            ch.link(dve.reduce_sum(nbl[:, :], nbv[:, :, :].rearrange("p b e -> p e b"), AXX))
            ch.link(dve.tensor_tensor_scan(bend[:, :], onesf[:, :], nbl[:, :], 0.0, ALU.mult, ALU.add))
            ch.link(dve.tensor_tensor(bst[:, :], bend[:, :], nbl[:, :], ALU.subtract))
            ch.link(dve.tensor_scalar(bst[:, :], bst[:, :], float(P), None, ALU.mult))
            ch.link(dve.tensor_tensor(rank[:, :, :], bank[1][:, 0:128].rearrange("p (t e) -> p t e", e=NE),
                                      bc(bst[:, :], [P, TT, NE], 1), ALU.add))
            ch.link(dve.tensor_tensor(dtmp[:, :, :, :], OH[:, :, :, :],
                                      rank[:, :, :].unsqueeze(2).to_broadcast([P, TT, TOPK, NE]), ALU.mult))
            ch.link(dve.reduce_sum(dest[:, :], dtmp[:, :, :, :].rearrange("p t k e -> p (t k) e"), AXX))
            NP = TT * TOPK
            ch.link(dve.tensor_scalar(destb[:, :], dest[:, :], 1.0 / P, -(P - 1) / (2.0 * P), ALU.mult, ALU.add))
            for shift in (1.5 * 2.0 ** 23, -1.5 * 2.0 ** 23):
                ch.link(dve.tensor_scalar(destb[:, :], destb[:, :], shift, None, ALU.add))
            ch.link(dve.scalar_tensor_tensor(destr[:, :], destb[:, :], -float(P), dest[:, :], ALU.mult, ALU.add))
            dve.tensor_tensor(ohR[:, :, :], bc(destr[:, :], [P, NP, P], 2), bc(iotaR[:, :], [P, NP, P], 1), ALU.is_equal)
            ch.link(dve.tensor_tensor(dcmp[:, :, :], bc(destb[:, :], [P, NP, NBT], 2), bc(iotaB[:, :], [P, NP, NBT], 1),
                                      ALU.is_equal))
            for v in range(3):
                ins = dve.tensor_tensor(rhsv[:, v], dcmp[:, :, :], bc(pair_ids[:, v, :], [P, NP, NBT], 2), ALU.mult)
            ins.then_inc(S("pairs_ok"), 1)
            for c in range(6, 8):
                xring.make_lo(dve, MOE0 + c, c)
            dve.wait_ge(S("slots_ps"), 1)
            sp_ = bank[3][:, 0:2 * NBT].rearrange("p (a b) -> p a b", a=2)
            ch.link(dve.tensor_copy(slotv[:, :, :], sp_))
            ch.link(dve.tensor_scalar(skipv[:, :], slotv[:, 1, :], 0.0, SKIP, ALU.is_equal, ALU.mult))
            dve.scalar_tensor_tensor(idx_x[:, :], slotv[:, 0, :], 0.25, skipv[:, :], ALU.mult, ALU.add)
            ch.link(dve.tensor_tensor(slotv[:, 0, :], slotv[:, 0, :], slotv[:, 1, :], ALU.add))
            ch.link(dve.scalar_tensor_tensor(idx_y[:, :], slotv[:, 0, :], -1.0, skipv[:, :], ALU.add, ALU.add))
            dve.sem_inc(S("slots_ok"), 1)
            ch.link(dve.tensor_tensor(ecmp[:, :, :], bc(iotaB[:, :], [P, NBT, NE], 2), bc(bend[:, :], [P, NBT, NE], 1),
                                      ALU.is_ge))
            ch.link(dve.reduce_sum(bef[:, :], ecmp[:, :, :], AXX))
            ch.link(dve.tensor_scalar(bef[:, :], bef[:, :], float(NE - 1), None, ALU.min))
            dve.tensor_copy(blk_exp[:, :], bef[:, :])
            dve.tensor_scalar(expsel[:, :], bef[0:96, :], lane32[0:96, :], None, ALU.is_equal)
            dve.tensor_copy(n_blk[:, 0:1], bend[:, NE - 1:NE])
            dve.tensor_scalar(n_blk[:, 1:2], bend[:, NE - 1:NE], -1.0, None, ALU.add)\
                .then_inc(S("tables_ok"), 1)

            dve.wait_ge(S("tables_ok"), 1)
            nb = dve.value_load(n_blk[0:1, 0:1], min_val=NE, max_val=NB - 1)
            last_blk = dve.value_load(n_blk[0:1, 1:2], min_val=NE - 1, max_val=NB - 2)
            xT_lo(dve, 0, 0)
            gate_part(dve, 0)
            block_dve(dve, 0, 0)
            block_dve(dve, 1, 1)
            with dve.Fori(0, (NB - 2) // 2) as it:
                for q in range(2):
                    i = it * 2 + (2 + q)
                    with dve.If(i < last_blk):
                        block_dve(dve, i, q)
                    with dve.If(i == last_blk):
                        block_dve(dve, i, q, final=True)
            dve.wait_ge(S("y_stored"), nb * 16)
            for tt in range(TT + 1):
                if tt < TT:
                    for k in range(TOPK):
                        if k % 2 == 0:
                            dve.wait_ge(S(f"y_pairs_in{tt % 2}{k // 2}"), 16 * (tt // 2 + 1))
                        ins = dve.scalar_tensor_tensor(H[:, tt, :], YG[:, tt % 2, k, :], gates[:, tt, k:k + 1], H[:, tt, :],
                                                       ALU.mult, ALU.add)
                        if k < TOPK - 1:
                            ch.link(ins)
                    ins.then_inc(S("combined"), 1)
                if tt >= 1:
                    t = tt - 1
                    dve.wait_ge(S("squares_ok"), t + 3)
                    dve.tensor_scalar(ss[:, 8 + t:9 + t], ss[:, 8 + t:9 + t], 1.0 / D, EPS, ALU.mult, ALU.add)\
                        .then_inc(S("ms_ok"), 1)
                    dve.wait_ge(S("rms_ok"), t + 3)
                    dve.wait_ge(S("g_fin_in"), 16)
                    if t >= 2:
                        dve.wait_ge(S("final_free"), t - 1)
                    dve.scalar_tensor_tensor(FO[:, t % 2, :], H[:, t, :], rms[:, 8 + t:9 + t], g_fin[:, :],
                                             ALU.mult, ALU.mult).then_inc(S("final_ok"), 1)

        def att_flip(pe, qt, pe_probs):
            pe.wait_ge(S("att_on"), qt + 1)
            pe.wait_ge(S("probsT_ok"), pe_probs)
            on = ON[:, :, :].rearrange("p h d -> p (h d)")
            for c in range(4):
                last = pe.matmul(bank[4][:, c * P:(c + 1) * P], on[:, c * P:(c + 1) * P], ident[:, :],
                                 start=True, stop=True, is_transpose=True)
            last.then_inc(S("attT_ps"), 1)

        @block.tensor
        def _(pe):
            def flip(o, i, n=P):
                return pe.matmul(o, i, ident[0:n, 0:n], start=True, stop=True, is_transpose=True)

            pe.wait_ge(S("ident_ok"), 1)
            pe.wait_ge(S("squares_ok"), 1)
            for tt in range(TT):
                pe.wait_ge(S("xs_ok"), tt + 1)
                for k in range(KT):
                    last = flip(bank[k][:, tt * P:(tt + 1) * P], xs[:, tt % 2, k::KT])
                last.then_inc(S("xT_first"), 1)

            pe.wait_ge(S("xnl_ok"), KT)
            pe.wait_ge(S("params_in"), 16 * NPAR)
            flip(bank[7][:, 0:48], par_rows[:, :], 48).then_inc(S("param_ps"), 1)
            for g in range(6):
                b0 = (g % 2) * 4
                if g == 1:
                    pe.wait_ge(S("params_ok"), 1)
                if g in (2, 4):
                    pe.wait_ge(S("qv_out"), g // 2)
                if g == 3:
                    pe.wait_ge(S("group1_out"), 1)
                if g == 5:
                    pe.wait_ge(S("unshifted_ok"), 4)
                for q in range(4):
                    n = 4 * g + q
                    pe.wait_ge(lo_done, n + 1)
                    wh = whi[:, n % NHL, :].rearrange("p (k n) -> p k n", k=2)
                    wl = wlo[:, n % NHL, :].rearrange("p (k n) -> p k n", k=2)
                    for c in range(4):
                        for j in range(2):
                            k = 2 * q + j
                            start, stop = k == 0, k == KT - 1
                            cs = slice(c * P, (c + 1) * P)
                            if g == 2:
                                last = three(pe, bank[b0 + c], wh[:, j, :], wl[:, j, :], xnh[:, k, cs], xnl[:, k, cs],
                                             start, stop, True)
                            else:
                                last = three(pe, bank[b0 + c], wh[:, j, cs], wl[:, j, cs], xnh[:, k, :], xnl[:, k, :],
                                             start, stop, False)
                    last.then_inc(w_used, 1)
            pe.wait_ge(S("unshifted_ok"), 8)
            for q in range(2):
                n = 24 + q
                pe.wait_ge(lo_done, n + 1)
                wh = whi[:, n % NHL, 0:640].rearrange("p (k n) -> p k n", k=4)
                wl = wlo[:, n % NHL, 0:640].rearrange("p (k n) -> p k n", k=4)
                for o, cs in ((bank[0], slice(0, P)), (bank[1][0:96, :], slice(64, 160))):
                    for j in range(4):
                        k = 4 * q + j
                        last = three(pe, o, wh[:, j, cs], wl[:, j, cs], xnh[:, k, :], xnl[:, k, :], k == 0, k == KT - 1,
                                     False)
                last.then_inc(w_used, 1)

            pe.wait_ge(S("unshifted_ok"), 14)
            pe.wait_ge(S("group1_out"), 1)
            pe.wait_ge(S("qv_out"), 2)
            for u in range(16 + 3):
                if u < 16:
                    qt, h = u // 4, u % 4
                    nk = (qt + 1) * P
                    if u >= 2:
                        pe.wait_ge(S("scores_ok"), u - 1)
                    for j in range(2):
                        r = slice(64 * j, 64 * j + 64)
                        last = pe.matmul(bank[2 * (u % 2) + j][:, 0:nk], QT[r, h, qt * P:(qt + 1) * P], KTT[r, h, 0:nk],
                                         start=True, stop=True)
                    last.then_inc(S("scores_ps"), 1)
                if u >= 3:
                    v = u - 3
                    qt = v // 4
                    pe.wait_ge(S("probsT_ok"), v + 1)
                    if v % 4 == 0 and qt >= 2:
                        pe.wait_ge(S("att_on"), qt - 1)
                    for j in range(2):
                        h = 2 * (v % 4) + j
                        for c in range(qt + 1):
                            last = pe.matmul(bank[6 + qt % 2][:, h * HD:(h + 1) * HD], PRT[:, v % 2, j, c * P:(c + 1) * P],
                                             VA[:, c, h * HD:(h + 1) * HD], start=c == 0, stop=c == qt)
                    last.then_inc(S("att_pv"), 1)
                if 2 <= u < 18:
                    v = u - 2
                    pe.wait_ge(S("probs_ok"), v + 1)
                    if v >= 1:
                        pe.wait_ge(S("probsT_ok"), v)
                    if v % 4 == 3 and v > 4:
                        att_flip(pe, v // 4 - 1, v)
                        pe.wait_ge(S("att_gained"), v // 4)
                    for j in range(2):
                        for c in range(v // 4 + 1):
                            last = flip(bank[4 + j][:, c * P:(c + 1) * P], PR[:, v % 2, j, c * P:(c + 1) * P])
                    last.then_inc(S("probsT_ps"), 1)

            pe.wait_ge(S("lora_in"), 1)
            pe.wait_ge(S("scores_ok"), 16)
            for h in range(HP):
                pe.matmul(bank[h], w2a2[0:32, h * P:(h + 1) * P], TL[:, :], start=True, stop=True)\
                    .then_inc(S("lora_ps"), 1)
            att_flip(pe, 3, 16)

            def norm_sums(sq, b):
                for h in range(HP):
                    for tt in range(TT):
                        last = pe.matmul(bank[b][:, 8 * tt + 2 * h:8 * tt + 2 * h + 2], sq[:, h, tt * P:(tt + 1) * P],
                                         head_ones[:, 0:P:HD], start=True, stop=True)
                last.then_inc(S("norm_ps"), 1)

            def norm_spread(n, b):
                pe.wait_ge(S("norm_inv"), n + 1)
                for tt in range(TT):
                    last = flip(bank[b + 1][0:8, tt * P:(tt + 1) * P], NR[:, 8 * tt:8 * tt + 8])
                last.then_inc(S("normT_ps"), 1)
                pe.wait_ge(S("normT_ok"), n + 1)
                for h in range(HP):
                    pe.matmul(bank[b + h], sel_T[:, h * P:(h + 1) * P], (NRT0, NRT1)[n][:, :], start=True, stop=True)\
                        .then_inc(S("norm_bc"), 1)

            pe.wait_ge(S("kk_sq"), HP)
            norm_sums(T4, 5)
            pe.wait_ge(S("att_done"), 1)
            for h in range(HP):
                if h == 1:
                    pe.wait_ge(S("norm_in"), 1)
                cs = slice(h * P, (h + 1) * P)
                pe.matmul(bank[4 + h], w2a2[32:64, cs], XL[32:64, 0, :], start=True, stop=True).then_inc(S("lora_ps"), 1)
            pe.wait_ge(S("sig_ok"), HP)
            norm_spread(0, 0)
            pe.wait_ge(S("prep_done"), 1)
            pe.wait_ge(S("state_written"), 1)

            def tile_pe(tt):
                pe.wait_ge(S("ab_tile"), tt + 1)
                pe.wait_ge(S("kr_tile"), tt + 1)
                pe.wait_ge(S("v_tile"), tt + 1)
                for b, t in enumerate((ASt, BSt, KSt, VSt)):
                    for h in range(HP):
                        last = flip(bank[b][:, h * P:(h + 1) * P], t[:, h, :])
                last.then_inc(S("rows_ps"), 1)

                def products(banks, left, right):
                    for h in range(HP):
                        for j in range(2):
                            r = slice(64 * j, 64 * j + 64)
                            last = pe.matmul(bank[banks + j][:, h * P:(h + 1) * P], left[r, h, :], right[r, h, :],
                                             start=True, stop=True)
                    return last

                pe.wait_ge(S("rwkv_out"), tt + 1)
                products(4, BSt, ASt)
                pe.wait_ge(S("state_written"), tt * 2 + 1)
                products(6, ASt, BSt).then_inc(S("AT_ps"), 1)
                pe.wait_ge(S("a_rows"), tt + 1)
                pe.wait_ge(S("bkv_rows"), tt + 1)
                products(0, KSt, ASt)
                products(2, BSt, RSt).then_inc(S("TK_ps"), 1)
                pe.wait_ge(S("AT_ok"), tt + 1)
                pe.wait_ge(S("inv_ok"), tt * 12 + 2)
                products(4, KSt, RSt).then_inc(S("RK_ps"), 1)
                pe.wait_ge(S("bonus_prod"), tt + 1)
                pe.matmul(bank[6], head_ones[:, :], BP[:, :, :].rearrange("p h t -> p (h t)"), start=True, stop=True)\
                    .then_inc(S("bonus_ps"), 1)
                pe.wait_ge(S("TK_ok"), tt + 1)
                pe.wait_ge(S("RB_ok"), tt + 1)
                pe.wait_ge(S("RK_ok"), tt + 1)

                for l in range(1, 6):
                    for j in range(2):
                        pe.wait_ge(S("inv_ok"), tt * 12 + (2 * l + j - 1) if l > 1 else tt * 12 + 2)
                        for h in range(HP):
                            last = pe.matmul(bank[j][:, h * P:(h + 1) * P], AsT[:, j, h, :], Xi[:, j, h, :],
                                             start=True, stop=True)
                        last.then_inc(S("step_ps"), 1)
                    if l == 1:
                        pe.wait_ge(S("bonus_ok"), tt + 1)
                        for h in range(8):
                            last = pe.matmul(bank[6][:, h * CH:(h + 1) * CH], TKm[:, h % 2, h // 2, :],
                                             Vt[:, h * CH:(h + 1) * CH], start=True, stop=True)
                        last.then_inc(S("z0_ps"), 1)
                    for j in range(2):
                        pe.wait_ge(S("step_ok"), tt * 10 + (2 * (l - 1) + j + 1))
                        for h in range(HP):
                            if l < 5:
                                pe.matmul(bank[2 + j][:, h * P:(h + 1) * P], XiT[:, j, h, :], Pm[:, j, h, :],
                                          start=True, stop=True)
                            last = pe.matmul(bank[4 + j][:, h * P:(h + 1) * P], Pm[:, j, h, :], XiT[:, j, h, :],
                                             start=True, stop=True)
                        last.then_inc(S("inv_ps"), 1)
                pe.wait_ge(S("z0_rows"), tt + 1)
                pe.wait_ge(S("inv_ok"), tt * 12 + 12)
                for h in range(8):
                    last = pe.matmul(bank[6 + h % 2][:, (h // 2) * P:(h // 2 + 1) * P], XiT[:, h % 2, h // 2, :],
                                     AZ[:, h, :, :].rearrange("p c d -> p (c d)"), start=True, stop=True)
                last.then_inc(S("uz_ps"), 1)
                pe.wait_ge(S("uz_rows"), tt + 1)
                for c in range(2):
                    r = slice(64 * c, 64 * c + 64)
                    for h in range(HP):
                        last = pe.matmul(bank[1 + c][:, h * P:(h + 1) * P], UZ[r, 0, 2 * h:2 * h + 2, :].rearrange("p h d -> p (h d)"),
                                         Bt[r, h * P:(h + 1) * P], start=True, stop=True)
                last.then_inc(S("map_ps"), 1)
                for h in range(8):
                    j = h % 2
                    last = pe.matmul(bank[0][64 * j:64 * j + 64, (h // 2) * P:(h // 2 + 1) * P], UZ[:, 0, h, :],
                                     RBm[:, j, h // 2, :], start=True, stop=True)
                last.then_inc(S("r2_ps"), 1)
                for c in range(2):
                    r = slice(64 * c, 64 * c + 64)
                    for h in range(HP):
                        o = bank[3 + c][:, h * P:(h + 1) * P]
                        pe.matmul(o, Bt[r, h * P:(h + 1) * P], UZ[r, 1, 2 * h:2 * h + 2, :].rearrange("p h d -> p (h d)"), start=True, stop=False)
                        last = pe.matmul(o, Kt[r, h * P:(h + 1) * P], Vt[r, h * P:(h + 1) * P], start=False, stop=True)
                last.then_inc(S("add_ps"), 1)
                for h in range(8):
                    j = h % 2
                    o = bank[5][64 * j:64 * j + 64, (h // 2) * P:(h // 2 + 1) * P]
                    pe.matmul(o, UZ[:, 1, h, :], RBm[:, j, h // 2, :], start=h < 2, stop=False, skip_group_check=True)
                    pe.matmul(o, Vt[:, h * CH:(h + 1) * CH], RKm[:, j, h // 2, :], start=False, stop=False,
                              skip_group_check=True)
                pe.wait_ge(S("r2_ok"), tt + 1)
                for c in range(2):
                    if c == 1:
                        pe.wait_ge(S("state_written"), tt * 2 + 2)
                    for h in range(HP):
                        last = pe.matmul(bank[5][:, h * P + 64 * c:h * P + 64 * c + 64], ST[:, h, :],
                                         R2[:, h, 64 * c:64 * c + 64], start=False, stop=c == 1, skip_group_check=True)
                    if c == 1:
                        last.then_inc(S("out_ps"), 1)
                    else:
                        pe.wait_ge(S("map_ok"), tt + 1)
                    for h in range(HP):
                        last = pe.matmul(bank[6 + c][:, h * P:(h + 1) * P], MTm[:, c, h, :], ST[:, h, :],
                                         start=True, stop=True)
                    last.then_inc(S("chain_ps"), 1)

            with pe.Fori(0, TT - 1) as tt:
                tile_pe(tt)
            tile_pe(TT - 1)

            pe.wait_ge(S("state_written"), 2 * TT + 1)
            pe.wait_ge(S("rwkv_out"), TT + 1)
            for h in range(HP):
                pe.matmul(bank[4 + h], head_ones[:, :], RX[:, h, :], start=True, stop=True).then_inc(S("gn_mean"), 1)
            for h in range(HP):
                pe.matmul(bank[h], g2[:, h * P:(h + 1) * P], XL[0:96, 1, :], start=True, stop=True)\
                    .then_inc(S("gate_ps"), 1)
            pe.wait_ge(S("gn_sq"), HP)
            pe.wait_ge(S("gn_centered"), HP)
            norm_sums(U2, 4)
            norm_spread(1, 4)
            pe.wait_ge(S("gn_normed"), HP)
            pe.wait_ge(S("gate_out"), HP)
            for c in range(OUT_CH):
                n = IN_CH + c
                pe.wait_ge(lo_done, n + 1)
                pe.wait_ge(S("mix_ok"), c + 1)
                for tt in range(TT):
                    for f in range(2):
                        ts, fs = slice(tt * P, (tt + 1) * P), slice(512 * f, 512 * f + 512)
                        last = three(pe, bank[2 * tt + f], whi[:, n % NHL, fs], wlo[:, n % NHL, fs], mxh[:, c, ts],
                                     mxl[:, c, ts], c == 0, c == OUT_CH - 1, True)
                last.then_inc(w_used, 1)

            pe.wait_ge(S("mix_added"), 8)
            for tt in range(TT):
                pe.wait_ge(S("xn2_ok"), tt + 1)
                for k in range(KT):
                    last = flip(bank[k][:, tt * P:(tt + 1) * P], XN2[:, tt, k::KT])
                last.then_inc(S("x2T_ps"), 1)
            for k in range(KT):
                pe.wait_ge(S("x2T_dve" if k % 2 else "x2T_act"), k // 2 + 1)
                for tt in range(TT):
                    last = pe.matmul(bank[0][:, tt * NE:(tt + 1) * NE], X2T[:, k, tt * P:(tt + 1) * P], w_rout[:, k, :],
                                     start=k == 0 and tt == 0, stop=k == KT - 1, skip_group_check=True)
            last.then_inc(S("logits_ps"), 1)
            pe.wait_ge(S("member_ok"), 1)
            for tt in range(TT):
                for t2 in range(tt + 1):
                    pe.matmul(bank[1][:, tt * NE:(tt + 1) * NE], (triu if t2 == tt else ones_b)[:, :], MB[:, t2, :],
                              start=t2 == 0, stop=t2 == tt)
            for tt in range(TT):
                last = pe.matmul(bank[2][:, 0:NE], ones_b[:, :], MB[:, tt, :], start=tt == 0, stop=tt == TT - 1)
            last.then_inc(S("rank_ps"), 1)
            pe.wait_ge(S("pairs_ok"), 1)
            NP = TT * TOPK
            for half, parts in ((0, (0, 1)), (1, (2,))):
                seq = [(v, m) for v in parts for m in range(NP)]
                for z, (v, m) in enumerate(seq):
                    last = pe.matmul(bank[3][:, half * NBT:(half + 1) * NBT], ohR[:, m, :], rhsv[:, v, m, :],
                                     start=z == 0, stop=z == len(seq) - 1)
            last.then_inc(S("slots_ps"), 1)


            def bias(o, w, f):
                return pe.matmul(o, bsel[:, :], biasb[:, w, 512 * f:512 * f + 512], start=True, stop=False)

            def chunk(n, k, o, xh, xl, kt):
                pe.wait_ge(lo_done, n + 1)
                for f in range(2):
                    fs = slice(512 * f, 512 * f + 512)
                    last = three(pe, o[:, fs], whi2[:, k % NHL2, fs], wlo2[:, k % NHL2, fs], xh[:, kt, :], xl[:, kt, :],
                                 False, kt == KT - 1, True)
                last.then_inc(w_used, 1)

            def block_transpose(src, done):
                for k in range(KT):
                    last = flip(bank[6 + k // 4][:, (k % 4) * P:(k % 4 + 1) * P], src[:, k::KT])
                last.then_inc(done, 1)

            pe.wait_ge(S("xb_in0"), 16)
            block_transpose(XB[:, 0, :], S("xT_ps"))
            pe.wait_ge(S("bias_sel"), 1)
            for f in range(2):
                last = bias(bank[f], 0, f)
            for c in range(8):
                if c == 0:
                    pe.wait_ge(S("xT_ok"), 1)
                chunk(MOE0 + c, c, pair[0], xbh[0], xbl[0], c)
            pe.wait_ge(S("tables_ok"), 1)
            last_blk = pe.value_load(n_blk[0:1, 1:2], min_val=NE - 1, max_val=NB - 2)

            def xb_turn(j, q):
                return (j // 2 + 1) if isinstance(j, int) else (j + (1 if q else 2)) // 2

            def block_pe(i, q, prev, final=False):
                base, k0 = MOE0 + 8 + i * PER, 8
                if prev is not None:
                    pe.wait_ge(S("up_ok"), i)
                for f in range(2):
                    bias(bank[2 + f], 1, f)
                for c in range(8):
                    chunk(base + c, k0 + c, pair[1], xbh[q], xbl[q], c)
                    if c == 2:
                        if prev is not None:
                            pe.wait_ge(S("y_act"), i)
                        for f in range(2):
                            last = bias(bank[4 + f], 2, f)
                        last.then_inc(S("up_down_bias"), 1)
                    if c == 3 and not final:
                        pe.wait_ge(S(f"xb_in{1 - q}"), xb_turn(i + 1, 1 - q) * 16)
                        if prev is not None:
                            pe.wait_ge(S("hT_ok"), i)
                        block_transpose(XB[:, 1 - q, :], S("xT_ps"))
                if final:
                    pe.wait_ge(S("hT_ok"), i)
                    pe.wait_ge(S("h_ok"), i + 1)
                    block_transpose(HB[:, :], S("hT_ps"))
                else:
                    pe.wait_ge(S("gate_ok"), i + 1)
                    pe.wait_ge(S("bias_sel"), i + 2)
                    for f in range(2):
                        bias(bank[f], 0, f)
                    pe.wait_ge(S("xT_ok"), i + 2)
                    for c in range(8):
                        chunk(base + (8 + c), k0 + 8 + c, pair[0], xbh[1 - q], xbl[1 - q], c)
                        if c == 4:
                            pe.wait_ge(S("h_ok"), i + 1)
                            block_transpose(HB[:, :], S("hT_ps"))
                pe.wait_ge(S("hT_ok"), i + 1)
                d0 = 8 if final else 16
                for c in range(8):
                    chunk(base + (d0 + c), k0 + d0 + c, pair[2], hbh, hbl, c)

            block_pe(0, 0, None)
            block_pe(1, 1, 0)
            with pe.Fori(0, (NB - 2) // 2) as it:
                for q in range(2):
                    i = it * 2 + (2 + q)
                    with pe.If(i < last_blk):
                        block_pe(i, q, it * 2 + (1 + q))
                    with pe.If(i == last_blk):
                        block_pe(i, q, it * 2 + (1 + q), final=True)



_INS = ["x", "norm_mix_g", "w_in", "attn_norm_g", "rwkv_mu", "rwkv_w0", "rwkv_w2", "rwkv_a0", "rwkv_a2", "rwkv_g2",
        "rwkv_k_k", "rwkv_k_a", "rwkv_r_k", "rwkv_ln_g", "rwkv_ln_b", "w_out", "norm_ffn_g", "w_router", "b_router",
        "moe_w_gate", "moe_b_gate", "moe_w_up", "moe_b_up", "moe_w_down", "moe_b_down", "norm_final_g"]


def kernel(**inputs):
    import numpy as _np
    import concourse.bacc as _bacc
    from concourse import mybir as _mybir
    from concourse.bass_utils import run_bass_kernel_spmd as _run

    nc = _bacc.Bacc("TRN2", target_bir_lowering=False, num_devices=1)
    arrays, aps = {}, {}
    for name in _INS:
        a = _np.ascontiguousarray(inputs[name])
        arrays[f"in_{name}_dram"] = a
        aps[name] = nc.dram_tensor(f"in_{name}_dram", a.shape, _mybir.dt.from_np(a.dtype), kind="ExternalInput").ap()
    out = nc.dram_tensor("out_0_dram", (1, 512, 1024), _mybir.dt.float32, kind="ExternalOutput").ap()
    hymba_block(nc, aps, out)
    r = _run(nc, [arrays], core_ids=[0])
    return r.results[0]["out_0_dram"]
```
